# Optimizing a Trainium2 kernel written in Bass

```python
import math
import jax, jax.numpy as jnp
from jax import lax
import numpy as np

D_MODEL = 1024
BATCH = 1
SEQ = 512
DEPTH = 2

CHUNK = 64
Q_BLOCK = 128
HEAD_DIM = 64
N_HEADS_DIFF = 4
DIFF_V_DIM = 2 * HEAD_DIM
N_HEADS_SB = 8
N_HEADS_FOX = 8
W_DIFF = N_HEADS_DIFF * DIFF_V_DIM
W_SB = N_HEADS_SB * HEAD_DIM
W_FOX = N_HEADS_FOX * HEAD_DIM
D_MIX = W_DIFF + W_SB + W_FOX
ROT_DIM = HEAD_DIM // 4
ROPE_THETA = 500000.0
NORM_EPS = 1e-6
IN_SPLITS = [W_DIFF, W_DIFF, W_DIFF, W_DIFF,
             W_SB, W_SB, W_SB, W_SB,
             W_FOX, W_FOX, W_FOX, W_FOX,
             N_HEADS_FOX]
D_IN = sum(IN_SPLITS)


def rms_norm(x, gain):
    xf = x.astype(jnp.float32)
    y = xf * lax.rsqrt(jnp.mean(xf * xf, axis=-1, keepdims=True) + NORM_EPS)
    return (y * gain.astype(jnp.float32)).astype(x.dtype)

def rope_tables(seq):
    pos = jnp.arange(seq, dtype=jnp.float32)
    inv_freq = ROPE_THETA ** (-jnp.arange(0, ROT_DIM, 2, dtype=jnp.float32) / ROT_DIM)
    ang = pos[:, None] * inv_freq[None, :]
    return jnp.cos(ang), jnp.sin(ang)

def apply_partial_rope(t, cos, sin):
    rot, rest = t[..., :ROT_DIM], t[..., ROT_DIM:]
    r1, r2 = rot[..., :ROT_DIM // 2], rot[..., ROT_DIM // 2:]
    rot = jnp.concatenate([r1 * cos - r2 * sin, r2 * cos + r1 * sin], axis=-1).astype(t.dtype)
    return jnp.concatenate([rot, rest], axis=-1)

def diff_attention(q, k, v, lam, lambda_init, sub_gain):
    seq = q.shape[3]
    scale = q.shape[-1] ** -0.5
    chunk_id = jnp.arange(seq) // CHUNK
    outs = []
    for i in range(seq // Q_BLOCK):
        q0, q1 = i * Q_BLOCK, (i + 1) * Q_BLOCK
        s = jnp.einsum('bhcqd,bhckd->bhcqk', q[:, :, :, q0:q1], k[:, :, :, :q1]).astype(jnp.float32) * scale
        allowed = chunk_id[:q1][None, :] <= chunk_id[q0:q1][:, None]
        p = jax.nn.softmax(jnp.where(allowed, s, -jnp.inf), axis=-1)
        w = p[:, :, 0] - lam * p[:, :, 1]
        outs.append(jnp.einsum('bhqk,bhkd->bhqd', w, v[:, :, :q1].astype(jnp.float32)))
    o = jnp.concatenate(outs, axis=2)
    return rms_norm(o, sub_gain) * (1.0 - lambda_init)

def stick_breaking_attention(q, k, v):
    seq = q.shape[2]
    scale = q.shape[-1] ** -0.5
    pos = jnp.arange(seq)
    outs = []
    for i in range(seq // Q_BLOCK):
        q0, q1 = i * Q_BLOCK, (i + 1) * Q_BLOCK
        z = jnp.einsum('bhqd,bhkd->bhqk', q[:, :, q0:q1], k[:, :, :q1]).astype(jnp.float32) * scale
        strict = pos[:q1][None, :] < pos[q0:q1][:, None]
        log_keep = jnp.where(strict, jax.nn.log_sigmoid(-z), 0.0)
        log_rest = lax.cumsum(log_keep, axis=3, reverse=True) - log_keep
        a = jnp.where(strict, jnp.exp(jax.nn.log_sigmoid(z) + log_rest), 0.0)
        outs.append(jnp.einsum('bhqk,bhkd->bhqd', a, v[:, :, :q1].astype(jnp.float32)))
    return jnp.concatenate(outs, axis=2)

def forgetting_attention(q, k, v, cum_log_f):
    seq = q.shape[2]
    scale = q.shape[-1] ** -0.5
    pos = jnp.arange(seq)
    outs = []
    for i in range(seq // Q_BLOCK):
        q0, q1 = i * Q_BLOCK, (i + 1) * Q_BLOCK
        logits = jnp.einsum('bhqd,bhkd->bhqk', q[:, :, q0:q1], k[:, :, :q1]).astype(jnp.float32) * scale
        logits = logits + cum_log_f[:, :, q0:q1, None] - cum_log_f[:, :, None, :q1]
        causal = pos[:q1][None, :] <= pos[q0:q1][:, None]
        p = jax.nn.softmax(jnp.where(causal, logits, -jnp.inf), axis=-1)
        outs.append(jnp.einsum('bhqk,bhkd->bhqd', p, v[:, :, :q1].astype(jnp.float32)))
    return jnp.concatenate(outs, axis=2)

def hybrid_layer(x, w_in, f_bias, lam_vec, subln, w_out, g_pre, g_post, layer_idx, cos, sin):
    b, s, _ = x.shape
    dt = x.dtype
    h = rms_norm(x, g_pre)
    p = h @ w_in
    split_at = np.cumsum(IN_SPLITS)[:-1].tolist()
    qa, ka, va, ga, qs, ks, vs, gs, qf, kf, vf, gf, ff = jnp.split(p, split_at, axis=-1)

    def heads(t, n, d):
        return t.reshape(b, s, n, d).transpose(0, 2, 1, 3)

    def merge(t):
        return t.transpose(0, 2, 1, 3).reshape(b, s, -1).astype(dt)

    qa = apply_partial_rope(qa.reshape(b, s, N_HEADS_DIFF, 2, HEAD_DIM).transpose(0, 2, 3, 1, 4), cos, sin)
    ka = apply_partial_rope(ka.reshape(b, s, N_HEADS_DIFF, 2, HEAD_DIM).transpose(0, 2, 3, 1, 4), cos, sin)
    lambda_init = 0.8 - 0.6 * math.exp(-0.3 * layer_idx)
    lv = lam_vec.astype(jnp.float32)
    lam = jnp.exp(jnp.sum(lv[0] * lv[1])) - jnp.exp(jnp.sum(lv[2] * lv[3])) + lambda_init
    ya = merge(diff_attention(qa, ka, heads(va, N_HEADS_DIFF, DIFF_V_DIM), lam, lambda_init, subln))
    ya = ya * jax.nn.silu(ga)

    yb = merge(stick_breaking_attention(heads(qs, N_HEADS_SB, HEAD_DIM), heads(ks, N_HEADS_SB, HEAD_DIM),
                                        heads(vs, N_HEADS_SB, HEAD_DIM)))
    yb = yb * jax.nn.silu(gs)

    log_f = jax.nn.log_sigmoid((ff + f_bias).astype(jnp.float32)).transpose(0, 2, 1)
    cum_log_f = jnp.cumsum(log_f, axis=-1)
    yc = merge(forgetting_attention(heads(qf, N_HEADS_FOX, HEAD_DIM), heads(kf, N_HEADS_FOX, HEAD_DIM),
                                    heads(vf, N_HEADS_FOX, HEAD_DIM), cum_log_f))
    yc = yc * jax.nn.silu(gf)

    y = jnp.concatenate([ya, yb, yc], axis=-1) @ w_out
    return x + rms_norm(y, g_post)

def first_inputs(seed: int = 0) -> dict:
    key = jax.random.key(seed)
    ks = jax.random.split(key, 8)
    x = jax.random.normal(ks[0], (BATCH, SEQ, D_MODEL), jnp.float32)
    w_in = jax.random.normal(ks[1], (DEPTH, D_MODEL, D_IN), jnp.float32) * D_MODEL ** -0.5
    forget_bias = jax.random.uniform(ks[2], (DEPTH, N_HEADS_FOX), jnp.float32, minval=1.0, maxval=4.0)
    diff_lambda = 0.1 * jax.random.normal(ks[3], (DEPTH, 4, HEAD_DIM), jnp.float32)
    diff_subln = 1.0 + 0.02 * jax.random.normal(ks[4], (DEPTH, DIFF_V_DIM), jnp.float32)
    w_out = jax.random.normal(ks[5], (DEPTH, D_MIX, D_MODEL), jnp.float32) * D_MIX ** -0.5
    pre_norm = 1.0 + 0.02 * jax.random.normal(ks[6], (DEPTH, D_MODEL), jnp.float32)
    post_norm = 1.0 + 0.02 * jax.random.normal(ks[7], (DEPTH, D_MODEL), jnp.float32)
    return {"x": x, "w_in": w_in, "forget_bias": forget_bias, "diff_lambda": diff_lambda,
            "diff_subln": diff_subln, "w_out": w_out, "pre_norm": pre_norm, "post_norm": post_norm}

def first_block(x, w_in, forget_bias, diff_lambda, diff_subln, w_out, pre_norm, post_norm):
    cos, sin = rope_tables(x.shape[1])
    for l in range(DEPTH):
        x = hybrid_layer(x, w_in[l], forget_bias[l], diff_lambda[l], diff_subln[l], w_out[l],
                         pre_norm[l], post_norm[l], l, cos, sin)
    return x


DEPTH_2 = 1

D_RNN = 1024
N_LRU_BLOCKS = 16
LRU_BLOCK = D_RNN // N_LRU_BLOCKS
CONV_WIDTH = 4
LRU_C = 8.0
ATTN_GROUPS = ((128, 1), (512, 4), (2048, 16))
N_GROUPS = len(ATTN_GROUPS)
HEADS_PER_GROUP = 4
HEAD_DIM_2 = 128
ATTN_WIDTH = N_GROUPS * HEADS_PER_GROUP * HEAD_DIM_2
ATTN_OUT_WIDTH = HEADS_PER_GROUP * HEAD_DIM_2
ROPE_DIM = HEAD_DIM_2 // 4
N_BRANCHES = 2
D_FF = ((8 * D_MODEL // 3 + 255) // 256) * 256
IN_WIDTH = 2 * D_RNN + 3 * ATTN_WIDTH + N_BRANCHES * D_MODEL
EPS = 1e-6
NEG = -1e30


def rms_norm_2(x, g):
    xf = x.astype(jnp.float32)
    y = xf * lax.rsqrt(jnp.mean(xf * xf, axis=-1, keepdims=True) + EPS)
    return (y * g.astype(jnp.float32)).astype(x.dtype)

def causal_depthwise_conv(x, w, b):
    y = lax.conv_general_dilated(
        x, w[:, None, :].astype(x.dtype), window_strides=(1,),
        padding=((CONV_WIDTH - 1, 0),), dimension_numbers=('NWC', 'WIO', 'NWC'),
        feature_group_count=x.shape[-1])
    return y + b.astype(x.dtype)

def rg_lru(x, w_rg, b_rg, w_ig, b_ig, lam):
    B, S, _ = x.shape
    xf = x.astype(jnp.float32)
    xb = xf.reshape(B, S, N_LRU_BLOCKS, LRU_BLOCK)
    r = jax.nn.sigmoid(jnp.einsum('bsnc,ncd->bsnd', xb, w_rg.astype(jnp.float32)).reshape(B, S, D_RNN) + b_rg.astype(jnp.float32))
    i = jax.nn.sigmoid(jnp.einsum('bsnc,ncd->bsnd', xb, w_ig.astype(jnp.float32)).reshape(B, S, D_RNN) + b_ig.astype(jnp.float32))
    log_a = -LRU_C * r * jax.nn.softplus(-lam.astype(jnp.float32))
    a = jnp.exp(log_a)
    mult = jnp.sqrt(-jnp.expm1(2.0 * log_a))
    mult = jnp.where(jnp.arange(S)[None, :, None] == 0, 1.0, mult)
    u = mult * (i * xf)

    def combine(left, right):
        a1, b1 = left
        a2, b2 = right
        return a1 * a2, a2 * b1 + b2

    _, h = lax.associative_scan(combine, (a, u), axis=1)
    return h.astype(x.dtype)

def partial_rope(t, cos, sin):
    half = ROPE_DIM // 2
    t1 = t[..., :half]
    t2 = t[..., half:ROPE_DIM]
    return jnp.concatenate([t1 * cos - t2 * sin, t2 * cos + t1 * sin, t[..., ROPE_DIM:]], axis=-1)

def dilated_window_attention(q, k, v, window, dilation):
    B, S, H, Dh = q.shape
    w_sub = window // dilation
    L = -(-S // dilation)
    nb = -(-L // Q_BLOCK)
    Lp = nb * Q_BLOCK
    pad = Lp * dilation - S

    def to_blocks(t):
        t = jnp.pad(t.astype(jnp.float32), ((0, 0), (0, pad), (0, 0), (0, 0)))
        t = t.reshape(B, Lp, dilation, H, Dh).transpose(0, 2, 1, 3, 4)
        return t.reshape(B, dilation, nb, Q_BLOCK, H, Dh)

    def with_prev(t):
        prev = jnp.pad(t[:, :, :-1], ((0, 0), (0, 0), (1, 0), (0, 0), (0, 0), (0, 0)))
        return jnp.concatenate([prev, t], axis=3)

    qb = to_blocks(q)
    kb = with_prev(to_blocks(k))
    vb = with_prev(to_blocks(v))

    qi = jnp.arange(Q_BLOCK)[:, None]
    kj = jnp.arange(2 * Q_BLOCK)[None, :]
    diff = qi + Q_BLOCK - kj
    band = (diff >= 0) & (diff <= w_sub)
    has_prev = (jnp.arange(nb)[:, None, None] > 0) | (kj[None] >= Q_BLOCK)
    mask = band[None] & has_prev

    s = jnp.einsum('brnqhc,brnkhc->brnhqk', qb, kb)
    s = jnp.where(mask[None, None, :, None], s, NEG)
    m = jnp.max(s, axis=-1, keepdims=True)
    p = jnp.exp(s - m)
    den = jnp.sum(p, axis=-1, keepdims=True)
    o = jnp.einsum('brnhqk,brnkhc->brnqhc', p, vb) / jnp.swapaxes(den, 3, 4)
    lse = jnp.swapaxes((m + jnp.log(den))[..., 0], 3, 4)

    o = o.reshape(B, dilation, Lp, H, Dh).transpose(0, 2, 1, 3, 4).reshape(B, Lp * dilation, H, Dh)[:, :S]
    lse = lse.reshape(B, dilation, Lp, H).transpose(0, 2, 1, 3).reshape(B, Lp * dilation, H)[:, :S]
    return o, lse

def second_inputs(seed: int = 0) -> dict:
    key = jax.random.key(seed)
    ks = jax.random.split(key, 24)
    f32 = jnp.float32

    def nrm(k, shape, fan_in):
        return jax.random.normal(k, shape, f32) * (fan_in ** -0.5)

    def gain(k):
        return 1.0 + 0.02 * jax.random.normal(k, (DEPTH_2, D_MODEL), f32)

    x = jax.random.normal(ks[0], (BATCH, SEQ, D_MODEL), f32)
    offset = jax.random.randint(ks[1], (BATCH, 1), 0, 4096, dtype=jnp.int32)
    positions = offset + jnp.arange(SEQ, dtype=jnp.int32)[None, :]
    u = jax.random.uniform(ks[2], (DEPTH_2, D_RNN), f32, 0.9, 0.999)
    a_base = u ** (1.0 / LRU_C)
    lru_lambda = jnp.log(a_base) - jnp.log1p(-a_base)
    return {
        "x": x,
        "positions": positions,
        "pre_mix_norm": gain(ks[3]),
        "w_in": nrm(ks[4], (DEPTH_2, D_MODEL, IN_WIDTH), D_MODEL),
        "conv_w": nrm(ks[5], (DEPTH_2, CONV_WIDTH, D_RNN), CONV_WIDTH),
        "conv_b": 0.01 * jax.random.normal(ks[6], (DEPTH_2, D_RNN), f32),
        "w_rg": nrm(ks[7], (DEPTH_2, N_LRU_BLOCKS, LRU_BLOCK, LRU_BLOCK), LRU_BLOCK),
        "b_rg": 0.01 * jax.random.normal(ks[8], (DEPTH_2, D_RNN), f32),
        "w_ig": nrm(ks[9], (DEPTH_2, N_LRU_BLOCKS, LRU_BLOCK, LRU_BLOCK), LRU_BLOCK),
        "b_ig": 0.01 * jax.random.normal(ks[10], (DEPTH_2, D_RNN), f32),
        "lru_lambda": lru_lambda,
        "w_lru_proj": nrm(ks[11], (DEPTH_2, D_RNN, D_MODEL), D_RNN),
        "w_attn_proj": nrm(ks[12], (DEPTH_2, ATTN_OUT_WIDTH, D_MODEL), ATTN_OUT_WIDTH),
        "w_out": nrm(ks[13], (DEPTH_2, D_MODEL, D_MODEL), D_MODEL),
        "post_mix_norm": gain(ks[14]),
        "pre_ffn_norm": gain(ks[15]),
        "w_ffn_gate": nrm(ks[16], (DEPTH_2, D_MODEL, D_FF), D_MODEL),
        "w_ffn_up": nrm(ks[17], (DEPTH_2, D_MODEL, D_FF), D_MODEL),
        "w_ffn_down": nrm(ks[18], (DEPTH_2, D_FF, D_MODEL), D_FF),
        "post_ffn_norm": gain(ks[19]),
    }

def second_block(x, positions, pre_mix_norm, w_in, conv_w, conv_b, w_rg, b_rg, w_ig, b_ig,
              lru_lambda, w_lru_proj, w_attn_proj, w_out, post_mix_norm, pre_ffn_norm,
              w_ffn_gate, w_ffn_up, w_ffn_down, post_ffn_norm):
    B, S, _ = x.shape
    dt = x.dtype
    inv_freq = ROPE_THETA ** (-jnp.arange(0, ROPE_DIM, 2, dtype=jnp.float32) / ROPE_DIM)
    ang = positions.astype(jnp.float32)[..., None] * inv_freq
    cos = jnp.cos(ang)[:, :, None, :].astype(dt)
    sin = jnp.sin(ang)[:, :, None, :].astype(dt)
    split_at = np.cumsum([D_RNN, D_RNN, ATTN_WIDTH, ATTN_WIDTH, ATTN_WIDTH]).tolist()

    for l in range(DEPTH_2):
        h = rms_norm_2(x, pre_mix_norm[l])
        proj = h @ w_in[l].astype(dt)
        xr, gr, q, k, v, gates = jnp.split(proj, split_at, axis=-1)

        xr = causal_depthwise_conv(xr, conv_w[l], conv_b[l])
        xr = rg_lru(xr, w_rg[l], b_rg[l], w_ig[l], b_ig[l], lru_lambda[l])
        y_lru = (xr * jax.nn.gelu(gr)) @ w_lru_proj[l].astype(dt)

        q = q.reshape(B, S, N_GROUPS, HEADS_PER_GROUP, HEAD_DIM_2)
        k = k.reshape(B, S, N_GROUPS, HEADS_PER_GROUP, HEAD_DIM_2)
        v = v.reshape(B, S, N_GROUPS, HEADS_PER_GROUP, HEAD_DIM_2)
        q = partial_rope(q, cos[:, :, None], sin[:, :, None]) * (HEAD_DIM_2 ** -0.5)
        k = partial_rope(k, cos[:, :, None], sin[:, :, None])
        outs, lses = [], []
        for g, (window, dilation) in enumerate(ATTN_GROUPS):
            o_g, lse_g = dilated_window_attention(q[:, :, g], k[:, :, g], v[:, :, g], window, dilation)
            outs.append(o_g)
            lses.append(lse_g)
        o = jnp.stack(outs, axis=2)
        wts = jax.nn.softmax(jnp.stack(lses, axis=2), axis=2)
        o = jnp.sum(wts[..., None] * o, axis=2).reshape(B, S, ATTN_OUT_WIDTH).astype(dt)
        y_attn = o @ w_attn_proj[l].astype(dt)

        g_lru, g_attn = jnp.split(jax.nn.sigmoid(gates), N_BRANCHES, axis=-1)
        mix = (g_lru * y_lru + g_attn * y_attn) @ w_out[l].astype(dt)
        x = x + rms_norm_2(mix, post_mix_norm[l])

        h = rms_norm_2(x, pre_ffn_norm[l])
        f = (jax.nn.silu(h @ w_ffn_gate[l].astype(dt)) * (h @ w_ffn_up[l].astype(dt))) @ w_ffn_down[l].astype(dt)
        x = x + rms_norm_2(f, post_ffn_norm[l])
    return x


def setup_inputs(seed=0):
    out = dict(first_inputs(seed))
    for name, value in second_inputs(seed + 1).items():
        if name != "x":
            out[name + "_2"] = value
    return out


def reference(
    x, w_in, forget_bias, diff_lambda, diff_subln, w_out, pre_norm, post_norm, positions_2,
    pre_mix_norm_2, w_in_2, conv_w_2, conv_b_2, w_rg_2, b_rg_2, w_ig_2, b_ig_2, lru_lambda_2,
    w_lru_proj_2, w_attn_proj_2, w_out_2, post_mix_norm_2, pre_ffn_norm_2, w_ffn_gate_2,
    w_ffn_up_2, w_ffn_down_2, post_ffn_norm_2,
):
    x = first_block(
        x, w_in, forget_bias, diff_lambda, diff_subln, w_out, pre_norm, post_norm,
    )
    return second_block(
        x, positions_2, pre_mix_norm_2, w_in_2, conv_w_2, conv_b_2, w_rg_2, b_rg_2, w_ig_2,
        b_ig_2, lru_lambda_2, w_lru_proj_2, w_attn_proj_2, w_out_2, post_mix_norm_2,
        pre_ffn_norm_2, w_ffn_gate_2, w_ffn_up_2, w_ffn_down_2, post_ffn_norm_2,
    )


_drawn_inputs = setup_inputs


def setup_inputs(seed=0):
    import zlib

    import numpy as np

    out = dict(_drawn_inputs(seed))
    spreads = {}
    factors = {'diff_subln': 2.907,
     'pre_mix_norm_2': 3.445,
     'b_rg_2': 38.574,
     'b_ig_2': 27.355,
     'post_mix_norm_2': 5.13,
     'pre_ffn_norm_2': 12.353,
     'post_ffn_norm_2': 55.121,
     'conv_b_2': 4.478}
    for name, (base, spread) in spreads.items():
        noise = np.random.default_rng([zlib.crc32(name.encode()), seed]).standard_normal(out[name].shape)
        drawn = base * np.exp(spread * noise) if base else spread * noise
        out[name] = __import__('jax').numpy.asarray(drawn.astype(out[name].dtype))
    for name, factor in factors.items():
        out[name] = (out[name] * factor).astype(out[name].dtype)
    return out
```

```python
import math

import numpy as np

import concourse.bass as bass
from concourse import mybir

S, D, P = 512, 1024, 128
TT, DC = S // P, D // P
DEPTH, HD = 2, 64
KINDS = ("diff", "sb", "fox")
ROT1, ROT2 = 16, 32
H2, G2 = 4, 3
D_FF = 2816
FC = D_FF // P
NEG = -1e30
EPS = 1e-6
BC = 2
COLS = 512
RAW, SPL = 3, 3
LAM_INIT = [0.8 - 0.6 * math.exp(-0.3 * l) for l in range(DEPTH)]
S0, S1, BT, BO = 4, 5, 6, 7
MASKS = ("causal", "strict", "chunk", "prev", "mod4d", "mod4", "mod16d", "mod16")


def plan():
    groups, steps, blocks = [], [], []

    def dense(tag, rows, orient, **more):
        g = dict(tag=tag, n=rows // BC, orient=orient, index=len(groups), first=len(blocks), **more)
        groups.append(g)
        out = []
        for k in range(g["n"]):
            out.append(("block", len(blocks), len(groups) - 1, k))
            blocks.append((len(groups) - 1, k))
        out.append(("drain", len(groups) - 1))
        return out

    def weave(blk, att):
        nb = sum(1 for s in blk if s[0] == "block")
        out, done, seen = [], 0, 0
        for s in blk:
            out.append(s)
            if s[0] == "block":
                seen += 1
            while s[0] != "block" or True:
                if done < len(att) and done < (seen * len(att)) / max(nb, 1) and s[0] != "drain":
                    out.append(att[done]); done += 1
                else:
                    break
        return out + att[done:]

    def attention(l, kind, n=16):
        return [("att", l, kind, s) for s in range(n + 2)]

    for l in range(DEPTH):
        steps.append(("norm", l, 0))
        steps.append(("forget", l))
        for ki, kind in enumerate(KINDS):
            o = "tok" if kind == "diff" else "feat"
            steps += dense("q", DC, o, l=l, kind=kind, ki=ki)
            steps += [("rope", len(groups) - 1)] if kind == "diff" else []
            steps += dense("k", DC, o, l=l, kind=kind, ki=ki)
            steps += [("rope", len(groups) - 1)] if kind == "diff" else []
            steps += dense("v", DC, "tok", l=l, kind=kind, ki=ki)
            steps += dense("g", DC, "feat", l=l, kind=kind, ki=ki)
            steps += attention(l, kind)
            for m in range(2):
                steps += dense("o", 4, "tok", l=l, kind=kind, ki=ki, m=m)
        steps.append(("post", l))
    steps.append(("norm", 2, 0))
    steps.append(("spill",))
    for m in range(2):
        steps += dense("xr", DC, "feat", m=m)
    for m in range(2):
        steps += dense("gr", DC, "feat", m=m)
    steps.append(("lru",))
    for m in range(2):
        steps += dense("gate", DC, "feat", m=m, which=0)
        steps += dense("mix", DC, "feat", m=m, which=0)
    steps.append(("angles",))
    for g in range(G2):
        for tag in ("q2", "k2"):
            steps += dense(tag, DC, "tok", g=g)
            steps += [("rope", len(groups) - 1)]
        steps += dense("v2", DC, "tok", g=g)
    steps += [("att", 2, "dil", s) for s in range(16 + 2)]
    for m in range(2):
        steps += dense("gate", DC, "feat", m=m, which=1)
        steps += dense("mix", 4, "feat", m=m, which=1)
    steps.append(("mixsplit",))
    for m in range(2):
        steps += dense("o2", DC, "tok", m=m)
    steps.append(("post", 2))
    steps.append(("norm", 3, 0))
    for m in range(FC // 2):
        steps += dense("ffn", DC, "feat", m=m)
    for m in range(2):
        steps += dense("down", FC, "tok", m=m)
    steps.append(("post", 3))

    used, full, use = [0] * 8, [0] * 8, {}
    maps = 0

    def take(key, bank, signal=True):
        use[key] = (bank, used[bank], full[bank] + 1 if signal else None)
        used[bank] += 1
        full[bank] += 1 if signal else 0

    marks, count = {}, {}

    def mark(name, key):
        count[name] = count.get(name, 0) + 1
        marks[name, key] = count[name]

    units = []
    for st in steps:
        if st[0] == "drain":
            for j in range(4):
                take(("dense", st[1], j), j, signal=j < 3)
        elif st[0] == "norm":
            for c in range(DC):
                take(("norm", st[1], c), 4 + c % 4)
        elif st[0] == "forget":
            take(("ff", st[1]), S0)
            take(("ffT", st[1]), S1)
        elif st[0] == "rope":
            for j in range(4):
                take(("rope", st[1], j), 4 + j)
        elif st[0] == "lru":
            for c in range(DC):
                take(("r", c), 4 + 2 * (c % 2))
                take(("i", c), 5 + 2 * (c % 2))
        elif st[0] == "att":
            _, l, kind, n = st
            if n < 16:
                units.append((l, kind, n))
                if kind in ("diff", "fox"):
                    for a in range(2):
                        mark("rows_max", (l, kind, n, a))
                if kind == "dil":
                    mark("rows_max", (l, kind, n, 0))
                if kind == "sb":
                    for a in range(2):
                        mark("abs_log", (l, kind, n, a))
                        mark("soft", (l, kind, n, a))
                if kind == "diff":
                    mark("soft", (l, kind, n, 0))
                    mark("rms", (l, kind, n))
            if n >= 2 and (n - 2) % 4 == 3:
                mark("y_high", (l, kind, (n - 2) // 4))
                mark("y_low", (l, kind, (n - 2) // 4))
            for a in unit_maps(kind) if n < 16 else ():
                take(("S", l, kind, n, a), (S0, S1, 3)[a])
            if 1 <= n <= 16:
                for a in value_maps(kind):
                    take(("T", l, kind, n - 1, a), BT)
                    use[("map", l, kind, n - 1, a)] = maps
                    maps += 1
                take(("O", l, kind, n - 1), BO, signal=False)
            if n >= 2 and (n - 2) % 4 == 3:
                take(("Y", l, kind, (n - 2) // 4), BT)
    return steps, groups, blocks, use, marks


def unit_maps(kind):
    return range(3 if kind == "dil" else 2)


def value_maps(kind):
    return {"diff": range(1), "dil": range(3)}.get(kind, range(2))


STEPS, GROUPS, BLOCKS, USE, MARKS = plan()
NB = len(BLOCKS)


def build(nc, x, wstream, w_ff, f_bias, lam_vec, subln, gains, post_gains, masks, ident_in, sel_in, rope1, positions,
          inv_freq, conv_w, conv_b, w_gates, b_gates, lru_lambda, x_spill, out):
    f32, f32r, bf16, i32 = mybir.dt.float32, mybir.dt.float32r, mybir.dt.bfloat16, mybir.dt.int32
    ALU, ACT, AX = mybir.AluOpType, mybir.ActivationFunctionType, mybir.AxisListType
    cursor = [(nc.sbuf_base + 63) // 64 * 64]

    def at(name, shape, dt, offset=None):
        size = int(np.prod(shape[1:])) * mybir.dt.size(dt)
        if offset is None:
            offset = cursor[0]
            cursor[0] += (size + 63) // 64 * 64
        return nc.alloc_sbuf_tensor_at(name, list(shape), dt, offset=offset)

    x_res = at("x_res", [P, TT, D], f32)
    mix = x_res[:, :, :].rearrange("p t (a s) -> p (t a) s", s=S)
    act_at = cursor[0]
    act_hl = at("act_hl", [P, DC, 2, S], f32r)
    y_ffn = at("y_ffn", [P, TT, D], f32, act_at)
    w_raw = at("w_raw", [P, RAW, BC * COLS], f32)
    w_hl = at("w_hl", [P, SPL, 2, BC, COLS], f32r)
    probs = at("probs", [P, 6, S], f32)
    tok_tmp = probs[:, 0:4, :]
    sig = probs[:, 0:4, :]
    probs_t = at("probs_t", [P, 2, S], f32)
    y_tok = at("y_tok", [P, 2, TT, P], f32)
    y_tmp = at("y_tmp", [P, S], f32)
    arena = cursor[0]
    y_hl = at("y_hl", [P, 4, 2, S], f32r)
    over = cursor[0]
    y_acc = at("y_acc", [P, TT, D], f32)
    gate = at("gate", [P, 4, S], f32)
    qT = at("qT", [P, 4, S], f32)
    kT = at("kT", [P, 4, S], f32)
    vv = at("vv", [P, TT, 4 * P], f32)
    sel_r = at("sel_r", [P, 8, P], f32r)
    ck = at("ck", [P, S], f32r)
    ckf = at("ckf", [P, S], f32)
    wff = at("wff", [P, DEPTH, DC, 8], f32)
    wff_hl = at("wff_hl", [P, 2, DC, 8], f32r)
    lv = at("lv", [P, DEPTH, 4, HD], f32)
    lru_am = at("lru_am", [P, DC, 2, S], f32, arena)
    lru_hl = at("lru_hl", [P, DC, 2, S], f32r, arena)
    PAD = 4
    xpad = at("xpad", [P, DC, PAD + S], f32, arena + 32768)
    xc = at("xc", [P, DC, S], f32, arena + 32768 + DC * (PAD + S) * 4)
    gelu = at("gelu", [P, DC, S], f32, arena + 49152 + DC * (PAD + S) * 4)
    q2 = at("q2", [P, G2 * H2, S], f32, over)
    k2 = at("k2", [P, G2 * H2, S], f32, over + 24576)
    v2 = at("v2", [P, TT, G2 * H2 * P], f32, over + 49152)
    hid_hl = at("hid_hl", [P, FC, 2, S], f32r, arena)
    cursor[0] = max(cursor[0], arena + FC * 2 * S * 4)
    mask_b = at("mask_b", [P, len(MASKS) + 1, P], bf16)
    ident = at("ident", [P, P], f32)
    sel = at("sel", [P, 8], f32)
    xpad0 = at("xpad0", [P, 1], f32)
    y_sq = at("y_sq", [P, P], f32)
    ones = at("ones", [P, 1], f32)
    eps = at("eps", [P, 1], f32)
    g_pre = at("g_pre", [P, 4, DC], f32)
    g_post = at("g_post", [P, D], f32)
    fb = at("fb", [P, DEPTH, 8], f32)
    sub_g = at("sub_g", [P, DEPTH], f32)
    rope_1 = at("rope_1", [P, 2, TT, ROT1 // 2], f32)
    rope_2 = at("rope_2", [P, 2, TT, ROT2 // 2], f32)
    ang = at("ang", [P, TT, ROT2 // 2], f32)
    red = at("red", [P, 2, TT, ROT2 // 2], f32)
    turns = at("turns", [P, 2, TT, ROT2 // 2], f32)
    posi = at("posi", [P, TT], i32)
    posf = at("posf", [P, TT], f32)
    invf = at("invf", [P, ROT2 // 2], f32)
    cw = at("cw", [P, DC, 4], f32)
    cb = at("cb", [P, DC], f32)
    wg = probs[:, 0:4, :].rearrange("p a (b n) -> p (a b) n", n=P)
    bg = at("bg", [P, 2, DC], f32)
    lam8 = at("lam8", [P, 3, DC], f32)
    stat = at("stat", [P, 64], f32)
    sums = at("sums", [P, 2, 4], f32)
    nmax = at("nmax", [P, 2, 4], f32)
    rinv = at("rinv", [P, 2, 4], f32)
    lam = at("lam", [P, 8], f32)
    ffs = at("ffs", [P, 3, TT, 8], f32)

    bank = [nc.alloc_psum_tensor(f"bank{i}", [P, S], f32) for i in range(8)]

    s_high_done = nc.alloc_semaphore("high_done")
    s_low_done = nc.alloc_semaphore("low_done")
    s_block_used = nc.alloc_semaphore("block_used")
    s_consts = nc.alloc_semaphore("consts")
    s_dve_step = nc.alloc_semaphore("dve_step")
    s_act_step = nc.alloc_semaphore("act_step")
    s_rows_max = nc.alloc_semaphore("rows_max")
    s_abs_log = nc.alloc_semaphore("abs_log")
    s_soft = nc.alloc_semaphore("soft")
    s_pv_done = nc.alloc_semaphore("pv_done")
    s_rms = nc.alloc_semaphore("rms")
    s_y_high = nc.alloc_semaphore("y_high")
    s_y_low = nc.alloc_semaphore("y_low")
    s_x_in = nc.alloc_semaphore("x_in")
    s_x_new = nc.alloc_semaphore("x_new")
    s_h_scale = nc.alloc_semaphore("h_scale")
    s_h_rows = nc.alloc_semaphore("h_rows")
    s_norm_high = nc.alloc_semaphore("norm_high")
    s_gain_in = nc.alloc_semaphore("gain_in")
    s_roped = nc.alloc_semaphore("roped")
    s_ff_split = nc.alloc_semaphore("ff_split")
    s_ff_log = nc.alloc_semaphore("ff_log")
    s_ff_keep = nc.alloc_semaphore("ff_keep")
    s_lam_dots = nc.alloc_semaphore("lam_dots")
    s_lam_exp = nc.alloc_semaphore("lam_exp")
    s_spilled = nc.alloc_semaphore("spilled")
    s_wg_in = nc.alloc_semaphore("wg_in")
    s_conv_done = nc.alloc_semaphore("conv_done")
    s_ix_done = nc.alloc_semaphore("ix_done")
    s_exp_done = nc.alloc_semaphore("exp_done")
    s_am_done = nc.alloc_semaphore("am_done")
    s_mult_done = nc.alloc_semaphore("mult_done")
    s_lru_val = nc.alloc_semaphore("lru_val")
    s_lru_high = nc.alloc_semaphore("lru_high")
    s_lru_low = nc.alloc_semaphore("lru_low")
    s_lam_log = nc.alloc_semaphore("lam_log")
    s_lam8_ready = nc.alloc_semaphore("lam8_ready")
    s_ang_ready = nc.alloc_semaphore("ang_ready")
    s_sin_done = nc.alloc_semaphore("sin_done")
    s_mix_high = nc.alloc_semaphore("mix_high")
    s_mix_low = nc.alloc_semaphore("mix_low")
    s_hid_val = nc.alloc_semaphore("hid_val")
    s_hid_high = nc.alloc_semaphore("hid_high")
    s_hid_low = nc.alloc_semaphore("hid_low")
    s_x_back = nc.alloc_semaphore("x_back")
    s_stored = nc.alloc_semaphore("stored")
    s_y_scale = nc.alloc_semaphore("y_scale")
    s_setup = nc.alloc_semaphore("setup")
    loaded = [nc.alloc_semaphore(f"loaded{i}") for i in range(RAW)]
    bank_full = [nc.alloc_semaphore(f"bank_full{i}") for i in range(8)]
    bank_free = [nc.alloc_semaphore(f"bank_free{i}") for i in range(8)]

    def full(key):
        return bank_full[USE[key][0]], USE[key][2]

    def drained(key):
        return bank_free[USE[key][0]], USE[key][1] + 1

    def earlier(key):
        return bank_free[USE[key][0]], USE[key][1]

    def tile_full(g, j):
        if j < 3:
            return full(("dense", g, j))
        return s_block_used, GROUPS[g]["first"] + GROUPS[g]["n"]

    def bank_of(key):
        return bank[USE[key][0]]

    def freed(key):
        return bank_free[USE[key][0]]

    def filled(key):
        return bank_full[USE[key][0]]

    def group(tag, **m):
        return next(g for g in GROUPS if g["tag"] == tag and all(g.get(k) == v for k, v in m.items()))

    def group_drained(g):
        return [drained(("dense", g["index"], j)) for j in range(4)]

    def group_turned(g):
        return [drained(("rope", g["index"], j)) for j in range(4)]

    def maps_before(l, kind):
        return USE[("map", l, kind, 0, 0)]


    def geometry(kind, a, i):
        first = max(i - 1, 0) if kind == "dil" and a == 0 else 0
        return first, i + 1 - first

    def mask_of(kind, a, i, kb):
        if kind == "dil":
            if a == 0:
                return "causal" if kb == i else "prev"
            return ("mod4", "mod16")[a - 1] + ("d" if kb == i else "")
        return {"diff": "chunk", "sb": "strict", "fox": "causal"}[kind] if kb == i else None

    def p_slot(kind, n, a):
        return (n % 2) * (3 if kind == "dil" else 2) + a

    def operand(g):
        if g["tag"] == "o" or (g["tag"] == "mix" and g["which"] == 1):
            return y_hl
        if g["tag"] == "mix":
            return lru_hl
        return hid_hl if g["tag"] == "down" else act_hl

    def qkv(l, kind):
        if kind == "dil":
            return q2, k2, v2
        return qT, kT, vv

    def blocks_before(tag, **m):
        return group(tag, **m)["first"]

    def pv_before(gi):
        n = 0
        for st in STEPS:
            if st == ("drain", gi):
                return n
            if st[0] == "att" and 1 <= st[3] <= 16:
                n += len(value_maps(st[2]))

    def prev_kind(l, kind):
        order = [(i, k) for i in range(DEPTH) for k in KINDS]
        return order[order.index((l, kind)) - 1]

    def norm_blocks(i):
        n = 0
        for st in STEPS:
            if st[:2] == ("norm", i):
                return n
            n += st[0] == "block"

    def o_end(l, kind):
        order = [(i, k) for i in range(DEPTH) for k in KINDS] + [(2, "dil")]
        pl, pk = order[order.index((l, kind)) - 1]
        g = group("o", l=pl, kind=pk, m=1)
        return g["first"] + g["n"]

    def ready(pe, l, kind):
        if kind == "dil":
            for g in range(G2):
                for done_tile in group_turned(group("q2", g=g)):
                    pe.wait_ge(*done_tile)
                for done_tile in group_turned(group("k2", g=g)):
                    pe.wait_ge(*done_tile)
                for done_tile in group_drained(group("v2", g=g)):
                    pe.wait_ge(*done_tile)
            return
        for tag in ("q", "k"):
            for done_tile in (group_turned if kind == "diff" else group_drained)(group(tag, l=l, kind=kind)):
                pe.wait_ge(*done_tile)
        for done_tile in group_drained(group("v", l=l, kind=kind)):
            pe.wait_ge(*done_tile)
        if kind == "fox":
            pe.wait_ge(*drained(("ffT", l)))

    def copy_turned(eng, engine, l, kind, n, a):
        _, nb = geometry(kind, a, n % 4)
        m = USE["map", l, kind, n, a]
        eng.wait_ge(*full(("T", l, kind, n, a)))
        ps = bank_of(("T", l, kind, n, a))
        if m - 1 > 0:
            eng.wait_ge(s_pv_done, m - 1)
        dst = probs_t[:, m % 2, 0:nb * P]
        op = engine.activation(dst, ps[:, 0:nb * P], ACT.Copy) if engine is nc.scalar else engine.tensor_copy(dst, ps[:, 0:nb * P])
        op.then_inc(freed(("T", l, kind, n, a)), 1)

    CONSTS = [(g_pre, gains), (mask_b, masks), (ident, ident_in), (sel, sel_in), (wff, w_ff),
              (fb, f_bias), (lv, lam_vec), (sub_g, subln), (rope_1, rope1), (posi, positions),
              (invf, inv_freq), (cw, conv_w), (cb, conv_b), (bg, b_gates), (lam8[:, 0], lru_lambda)]

    def whole(t):
        return t if isinstance(t, bass.AP) else t[tuple(slice(None) for _ in t.shape)]

    with nc.Block() as block:

        @block.sync
        def _(sp):
            sp.dma_start(x_res[:, :, :], x.rearrange("b (t p) d -> p (b t) d", p=P)).then_inc(s_x_in, 16)
            for dst, src in CONSTS:
                sp.dma_start(whole(dst), whole(src)).then_inc(s_consts, 16)
            for b in range(NB):
                if b - RAW + 1 > 0:
                    sp.wait_ge(s_low_done, b - RAW + 1)
                sp.dma_start(w_raw[:, b % RAW, :], wstream[b]).then_inc(loaded[b % RAW], 16)
            for t in range(TT):
                sp.wait_ge(s_x_new, 3 * TT + t + 1)
                sp.dma_start(out.rearrange("b (t p) d -> p (b t) d", p=P)[:, t, :], x_res[:, t, :]).then_inc(s_stored, 16)
            sp.wait_ge(s_stored, 16 * TT)

        @block.gpsimd
        def _(pool):
            for b in range(NB):
                pool.wait_ge(s_high_done, b + 1)
                w = w_raw[:, b % RAW, :]
                nc.gpsimd.tensor_tensor(
                    w_hl[:, b % SPL, 1].rearrange("p c n -> p (c n)"), w,
                    w_hl[:, b % SPL, 0].rearrange("p c n -> p (c n)").bitcast(f32),
                    ALU.subtract).then_inc(s_low_done, 1)

        @block.tensor
        def _(pe):
            def three(out_ap, hi, lo, feat, start, stop):
                (wh, wl), (ah, al) = hi, lo
                if feat:
                    pe.matmul(out_ap, wh, ah, start=start, stop=False)
                    pe.matmul(out_ap, wh, al, start=False, stop=False)
                    return pe.matmul(out_ap, wl, ah, start=False, stop=stop)
                pe.matmul(out_ap, ah, wh, start=start, stop=False)
                pe.matmul(out_ap, ah, wl, start=False, stop=False)
                return pe.matmul(out_ap, al, wh, start=False, stop=stop)

            def product(b, gi, k):
                g = GROUPS[gi]
                A, w = operand(g), w_hl[:, b % SPL]
                if k == 0:
                    if g["tag"] == "o":
                        pe.wait_ge(s_y_low, MARKS["y_low", (g["l"], g["kind"], 3)])
                    if g["tag"] == "mix":
                        if g["which"] == 0:
                            pe.wait_ge(s_lru_low, DC)
                        else:
                            pe.wait_ge(*drained(("Y", 2, "dil", 3)))
                    if g["tag"] == "o2":
                        pe.wait_ge(s_mix_low, DC)
                    if g["tag"] == "down":
                        pe.wait_ge(s_hid_low, FC)
                pe.wait_ge(s_low_done, b + 1)
                for j in range(4):
                    if k == 0:
                        if earlier(("dense", gi, j))[1] > 0:
                            pe.wait_ge(*earlier(("dense", gi, j)))
                    js = slice(j * P, (j + 1) * P)
                    for cc in range(BC):
                        c, feat = k * BC + cc, g["orient"] == "feat"
                        ws, as_ = (js, slice(None)) if feat else (slice(None), js)
                        mm = three(bank[j][:, :], (w[:, 0, cc, ws], w[:, 1, cc, ws]),
                                   (A[:, c, 0, as_], A[:, c, 1, as_]), feat,
                                   start=(c == 0), stop=(c == g["n"] * BC - 1))
                    if k == g["n"] - 1 and j < 3:
                        mm.then_inc(filled(("dense", gi, j)), 1)
                mm.then_inc(s_block_used, 1)

            def norm_turn(i):
                for c in range(DC):
                    if earlier(("norm", i, c))[1] > 0:
                        pe.wait_ge(*earlier(("norm", i, c)))
                    to = bank_of(("norm", i, c))
                    for t in range(TT):
                        if c == 0:
                            pe.wait_ge(s_h_rows, i * TT + t + 1)
                        tr = pe.transpose(to[:, t * P:(t + 1) * P], y_acc[:, t, c * P:(c + 1) * P], ident[:, :])
                    tr.then_inc(filled(("norm", i, c)), 1)
                for c in range(4, DC):
                    pe.wait_ge(*drained(("norm", i, c)))

            def forget(l):
                if earlier(("ff", l))[1] > 0:
                    pe.wait_ge(*earlier(("ff", l)))
                to = bank_of(("ff", l))
                pe.wait_ge(s_ff_split, l + 1)
                for t in range(TT):
                    for c in range(DC):
                        mm = three(to[:, t * 8:(t + 1) * 8], (wff_hl[:, 0, c], wff_hl[:, 1, c]),
                                   (act_hl[:, c, 0, t * P:(t + 1) * P], act_hl[:, c, 1, t * P:(t + 1) * P]),
                                   False, start=(c == 0), stop=(c == DC - 1))
                mm.then_inc(filled(("ff", l)), 1)
                if earlier(("ffT", l))[1] > 0:
                    pe.wait_ge(*earlier(("ffT", l)))
                to = bank_of(("ffT", l))
                pe.wait_ge(s_ff_keep, l + 1)
                for t in range(TT):
                    tr = pe.transpose(to[0:8, t * P:(t + 1) * P], ffs[:, 2, t, :], ident[:, :])
                tr.then_inc(filled(("ffT", l)), 1)

            def rope_turn(gi, nth):
                pe.wait_ge(s_roped, nth)
                for j in range(4):
                    if earlier(("rope", gi, j))[1] > 0:
                        pe.wait_ge(*earlier(("rope", gi, j)))
                    to = bank_of(("rope", gi, j))
                    for t in range(TT):
                        tr = pe.transpose(to[:, t * P:(t + 1) * P], tok_tmp[:, t, j * P:(j + 1) * P], ident[:, :])
                    tr.then_inc(filled(("rope", gi, j)), 1)

            def scores(l, kind, n):
                q, k, _ = qkv(l, kind)
                p, i = n // 4, n % 4
                for a in unit_maps(kind):
                    first, nb = geometry(kind, a, i)
                    if earlier(("S", l, kind, n, a))[1] > 0:
                        pe.wait_ge(*earlier(("S", l, kind, n, a)))
                    to = bank_of(("S", l, kind, n, a))
                    rows = slice(0, P) if kind == "dil" else slice(a * HD, (a + 1) * HD)
                    ch = a * H2 + p if kind == "dil" else p
                    pe.matmul(to[:, 0:nb * P], q[rows, ch, i * P:(i + 1) * P],
                              k[rows, ch, first * P:(first + nb) * P], start=True, stop=False)
                    if kind == "fox":
                        pe.matmul(to[:, 0:nb * P], sel_r[:, 2 * p + a, :], ck[:, 0:nb * P],
                                  start=False, stop=False)
                    masked = [kb for kb in range(first, first + nb) if mask_of(kind, a, i, kb)]
                    for kb in masked:
                        cols = slice((kb - first) * P, (kb - first + 1) * P)
                        mm = pe.matmul(to[:, cols], mask_b[:, len(MASKS), :],
                                       mask_b[:, MASKS.index(mask_of(kind, a, i, kb)), :],
                                       start=False, stop=(kb == masked[-1]))
                    mm.then_inc(filled(("S", l, kind, n, a)), 1)

            def values(l, kind, n):
                _, _, v = qkv(l, kind)
                p, i = n // 4, n % 4
                for a in value_maps(kind):
                    first, nb = geometry(kind, a, i)
                    if earlier(("T", l, kind, n, a))[1] > 0:
                        pe.wait_ge(*earlier(("T", l, kind, n, a)))
                    to = bank_of(("T", l, kind, n, a))
                    if kind in ("diff", "sb"):
                        pe.wait_ge(s_soft, MARKS["soft", (l, kind, n, a)])
                    else:
                        pe.wait_ge(*drained(("S", l, kind, n, a)))
                    for kb in range(nb):
                        tr = pe.transpose(to[:, kb * P:(kb + 1) * P],
                                          probs[:, p_slot(kind, n, a), kb * P:(kb + 1) * P], ident[:, :])
                    tr.then_inc(filled(("T", l, kind, n, a)), 1)
                if earlier(("O", l, kind, n))[1] > 0:
                    pe.wait_ge(*earlier(("O", l, kind, n)))
                to = bank_of(("O", l, kind, n))
                for a in value_maps(kind):
                    first, nb = geometry(kind, a, i)
                    pe.wait_ge(*drained(("T", l, kind, n, a)))
                    half = slice(a * HD, (a + 1) * HD) if kind in ("sb", "fox") else slice(0, P)
                    at_ = (a * H2 + p) * P if kind == "dil" else p * P + half.start
                    one = kind != "dil" or a == 0
                    end = kind != "dil" or a == 2
                    for kb in range(nb):
                        mm = pe.matmul(to[:, half], probs_t[:, USE["map", l, kind, n, a] % 2, kb * P:(kb + 1) * P],
                                       v[:, first + kb, at_:at_ + half.stop - half.start],
                                       start=(one and kb == 0), stop=(end and kb == nb - 1))
                    mm.then_inc(s_pv_done, 1)

            def heads_turn(l, kind, p):
                if earlier(("Y", l, kind, p))[1] > 0:
                    pe.wait_ge(*earlier(("Y", l, kind, p)))
                to = bank_of(("Y", l, kind, p))
                pe.wait_ge(*drained(("O", l, kind, 4 * p + 3)))
                for i in range(TT):
                    tr = pe.transpose(to[:, i * P:(i + 1) * P], y_tok[:, p % 2, i, :], ident[:, :])
                tr.then_inc(filled(("Y", l, kind, p)), 1)

            def gates(c):
                if c == 0:
                    pe.wait_ge(s_wg_in, 16)
                pe.wait_ge(s_conv_done, c + 1)
                for w, name in enumerate("ri"):
                    if earlier((name, c))[1] > 0:
                        pe.wait_ge(*earlier((name, c)))
                    to = bank_of((name, c))
                    pe.matmul(to[:, :], wg[:, w * DC + c, :], xc[:, c, :], start=True, stop=True)\
                        .then_inc(filled((name, c)), 1)

            pe.wait_ge(s_consts, 16 * len(CONSTS))
            ropes = 0
            for st in STEPS:
                if st[0] == "block":
                    product(*st[1:])
                elif st[0] == "norm":
                    norm_turn(st[1])
                elif st[0] == "forget":
                    forget(st[1])
                elif st[0] == "rope":
                    ropes += 1
                    rope_turn(st[1], ropes)
                elif st[0] == "lru":
                    for c in range(DC):
                        gates(c)
                elif st[0] == "att":
                    _, l, kind, n = st
                    if n == 0:
                        ready(pe, l, kind)
                    if n < 16:
                        scores(l, kind, n)
                    if 1 <= n <= 16:
                        values(l, kind, n - 1)
                    if n >= 2 and (n - 2) % 4 == 3:
                        heads_turn(l, kind, (n - 2) // 4)

        @block.scalar
        def _(act):
            step = [0]

            def link(ins):
                step[0] += 1
                ins.then_inc(s_act_step, 1)
                act.wait_ge(s_act_step, step[0])

            def high(b):
                if b >= NB:
                    return
                act.wait_ge(loaded[b % RAW], 16 * (b // RAW + 1))
                if b - SPL + 1 > 0:
                    act.wait_ge(s_block_used, b - SPL + 1)
                if b - SPL + 1 > 0:
                    act.wait_ge(s_low_done, b - SPL + 1)
                nc.scalar.activation(w_hl[:, b % SPL, 0].rearrange("p c n -> p (c n)"), w_raw[:, b % RAW, :],
                                     ACT.Copy).then_inc(s_high_done, 1)

            def norm(i):
                act.wait_ge(s_x_in, 16)
                if i == 0:
                    act.wait_ge(s_consts, 16 * len(CONSTS))
                    act.wait_ge(s_setup, 1)
                for t in range(TT):
                    if (i - 1) * TT + t + 1 > 0:
                        act.wait_ge(s_x_new, (i - 1) * TT + t + 1)
                    link(nc.scalar.activation(probs[:, 0:2, :].rearrange("p a s -> p (a s)"), x_res[:, t, :],
                                              ACT.Square, accum_out=stat[:, t:t + 1]))
                link(nc.scalar.activation(stat[:, 4:8], stat[:, 0:4], ACT.Ln, bias=eps[:, 0:1], scale=1.0 / D))
                nc.scalar.activation(stat[:, 8:12], stat[:, 4:8], ACT.Exp, scale=-0.5).then_inc(s_h_scale, 1)
                act.dma_start(g_post[:, :], post_gains[i:i + 1, :].partition_broadcast(P)).then_inc(s_gain_in, 16)
                for c in range(DC):
                    act.wait_ge(*full(("norm", i, c)))
                    t = bank_of(("norm", i, c))
                    if c == 0 and i > 0:
                        act.wait_ge(s_block_used, norm_blocks(i))
                    nc.scalar.activation(act_hl[:, c, 0, :], t[:, :], ACT.Copy, scale=g_pre[:, i, c:c + 1])\
                        .then_inc(s_norm_high, 1)

            def forget(l):
                act.wait_ge(*drained(("ff", l)))
                link(nc.scalar.activation(ffs[:, 1], ffs[:, 0], ACT.Abs))
                link(nc.scalar.activation(ffs[:, 1], ffs[:, 1], ACT.Exp, scale=-1.0))
                nc.scalar.activation(ffs[:, 1], ffs[:, 1], ACT.Ln, bias=ones[:, 0:1]).then_inc(s_ff_log, 1)
                act.wait_ge(s_lam_dots, l + 1)
                nc.scalar.activation(lam[:, 2:4], lam[:, 0:2], ACT.Exp).then_inc(s_lam_exp, 1)

            def drain(gi):
                g = GROUPS[gi]
                tag = g["tag"]
                if tag in ("o", "mix", "down"):
                    return
                if tag == "q" or tag == "v" or tag == "k":
                    act.wait_ge(s_pv_done, pv_before(gi))
                if tag in ("q", "k", "q2", "k2") and g["orient"] == "tok":
                    before = [x["index"] for x in GROUPS[:gi] if x["orient"] == "tok" and x["tag"] in ("q", "k", "q2", "k2")]
                    if before:
                        act.wait_ge(*full(("rope", before[-1], 3)))
                if tag == "g" and gi > 4:
                    act.wait_ge(s_y_low, MARKS["y_low", prev_kind(g["l"], g["kind"]) + (3,)])
                for j in range(4):
                    act.wait_ge(*tile_full(gi, j))
                    ps = bank[j]
                    done = freed(("dense", gi, j))
                    if tag in ("q", "k", "q2", "k2") and g["orient"] == "tok":
                        nc.scalar.activation(tok_tmp[:, j, :], ps[:, :], ACT.Copy).then_inc(done, 1)
                    elif tag == "q":
                        nc.scalar.activation(qT[:, j, :], ps[:, :], ACT.Copy, scale=HD ** -0.5).then_inc(done, 1)
                    elif tag == "k":
                        nc.scalar.activation(kT[:, j, :], ps[:, :], ACT.Copy).then_inc(done, 1)
                    elif tag == "v":
                        nc.scalar.activation(vv[:, j, :], ps[:, :], ACT.Copy).then_inc(done, 1)
                    elif tag == "v2":
                        nc.scalar.activation(v2[:, j, g["g"] * COLS:(g["g"] + 1) * COLS], ps[:, :], ACT.Copy).then_inc(done, 1)
                    elif tag == "g":
                        nc.scalar.activation(gate[:, j, :], ps[:, :], ACT.Silu).then_inc(done, 1)
                    elif tag == "xr":
                        nc.scalar.activation(xpad[:, 4 * g["m"] + j, PAD:], ps[:, :], ACT.Copy).then_inc(done, 1)
                    elif tag == "gr":
                        nc.scalar.activation(gelu[:, 4 * g["m"] + j, :], ps[:, :], ACT.Gelu_apprx_tanh).then_inc(done, 1)
                    elif tag == "gate":
                        if g["m"]:
                            act.wait_ge(*drained(("dense", gi - 1, j)))
                        nc.scalar.activation(sig[:, j, :], ps[:, :], ACT.Sigmoid).then_inc(done, 1)
                    elif tag == "o2":
                        nc.scalar.activation(y_acc[:, j, g["m"] * COLS:(g["m"] + 1) * COLS], ps[:, :], ACT.Copy).then_inc(done, 1)
                    elif tag == "ffn" and j < 2:
                        n = 2 * g["m"] + j
                        if n - 1 > 0:
                            act.wait_ge(s_hid_val, n - 1)
                        nc.scalar.activation(probs[:, j, :], ps[:, :], ACT.Silu).then_inc(done, 1)
                    elif tag == "ffn":
                        n = 2 * g["m"] + j - 2
                        act.wait_ge(s_hid_val, n + 1)
                        nc.scalar.activation(hid_hl[:, n, 0, :], probs[:, j, :], ACT.Copy).then_inc(s_hid_high, 1)

            def rope(gi):
                g = GROUPS[gi]
                for j in range(4):
                    act.wait_ge(*full(("rope", gi, j)))
                    ps = bank_of(("rope", gi, j))
                    scale = {"q": HD ** -0.5, "q2": (2 * HD) ** -0.5}.get(g["tag"], 1.0)
                    dst = {"q": qT, "k": kT, "q2": q2, "k2": k2}[g["tag"]]
                    nc.scalar.activation(dst[:, g.get("g", 0) * H2 + j, :], ps[:, :], ACT.Copy, scale=scale)\
                        .then_inc(freed(("rope", gi, j)), 1)

            def soften(l, kind, n):
                par = n % 2
                if n >= 2:
                    act.wait_ge(*full(("T", l, kind, n - 2, value_maps(kind)[-1])))
                for a in unit_maps(kind):
                    _, nb = geometry(kind, a, n % 4)
                    row = probs[:, p_slot(kind, n, a), 0:nb * P]
                    if kind == "sb":
                        act.wait_ge(*full(("S", l, kind, n, a)))
                        ps = bank_of(("S", l, kind, n, a))
                        link(nc.scalar.activation(row, ps[:, 0:nb * P], ACT.Abs))
                        link(nc.scalar.activation(row, row, ACT.Exp, scale=-1.0))
                        nc.scalar.activation(row, row, ACT.Ln, bias=ones[:, 0:1]).then_inc(s_abs_log, 1)
                    else:
                        if kind != "dil" or a == 0:
                            act.wait_ge(s_rows_max, MARKS["rows_max", (l, kind, n, a)])
                        b = 0 if kind == "dil" else a
                        nc.scalar.activation(row, bank[USE["S", l, kind, n, a][0]][:, 0:nb * P], ACT.Exp,
                                             bias=nmax[:, par, b:b + 1], accum_out=sums[:, par, a:a + 1])\
                            .then_inc(freed(("S", l, kind, n, a)), 1)
                if kind == "sb":
                    for a in range(2):
                        _, nb = geometry(kind, a, n % 4)
                        row = probs[:, p_slot(kind, n, a), 0:nb * P]
                        act.wait_ge(*drained(("S", l, kind, n, a)))
                        nc.scalar.activation(row, row, ACT.Exp).then_inc(s_soft, 1)

            def turned(l, kind, n):
                for a in value_maps(kind):
                    if a % 2 == 0:
                        copy_turned(act, nc.scalar, l, kind, n, a)
                if kind == "diff":
                    act.wait_ge(s_pv_done, USE["map", l, kind, n, 0] + 1)
                    link(nc.scalar.activation(y_sq[:, :], bank[BO][:, 0:P], ACT.Square, accum_out=stat[:, 16:17]))
                    link(nc.scalar.activation(stat[:, 17:18], stat[:, 16:17], ACT.Ln, bias=eps[:, 0:1], scale=1.0 / P))
                    nc.scalar.activation(stat[:, 18 + n % 2:19 + n % 2], stat[:, 17:18], ACT.Exp, scale=-0.5)\
                        .then_inc(s_rms, 1)

            def heads(l, kind, p):
                if kind == "dil":
                    act.wait_ge(*full(("Y", l, kind, p)))
                    ps = bank_of(("Y", l, kind, p))
                    src = ps[:, :]
                else:
                    act.wait_ge(*drained(("Y", l, kind, p)))
                    src = y_tmp[:, :]
                if p == 0 and (l, kind) != (0, KINDS[0]):
                    act.wait_ge(s_block_used, o_end(l, kind))
                nc.scalar.activation(y_hl[:, p, 0, :], src, ACT.Copy).then_inc(s_y_high, 1)

            def lru():
                link(nc.scalar.activation(lam8[:, 1], lam8[:, 0], ACT.Abs))
                link(nc.scalar.activation(lam8[:, 1], lam8[:, 1], ACT.Exp, scale=-1.0))
                nc.scalar.activation(lam8[:, 1], lam8[:, 1], ACT.Ln, bias=ones[:, 0:1]).then_inc(s_lam_log, 1)
                for c in range(DC):
                    act.wait_ge(*full(("r", c)))
                    ps = bank_of(("r", c))
                    nc.scalar.activation(xpad[:, c, PAD:], ps[:, :], ACT.Sigmoid, bias=bg[:, 0, c:c + 1])\
                        .then_inc(freed(("r", c)), 1)
                    act.wait_ge(*full(("i", c)))
                    ps = bank_of(("i", c))
                    if c - 1 > 0:
                        act.wait_ge(s_ix_done, c - 1)
                    nc.scalar.activation(probs[:, 4 + c % 2, :], ps[:, :], ACT.Sigmoid, bias=bg[:, 1, c:c + 1])\
                        .then_inc(freed(("i", c)), 1)
                act.wait_ge(s_lam8_ready, 1)
                act.wait_ge(*drained(("r", DC - 1)))
                act.wait_ge(*drained(("r", DC - 2)))
                for c in range(DC):
                    nc.scalar.activation(lru_am[:, c, 1, :], xpad[:, c, PAD:], ACT.Tanh, scale=lam8[:, 2, c:c + 1])
                    nc.scalar.activation(lru_am[:, c, 0, :], xpad[:, c, PAD:], ACT.Exp, scale=lam8[:, 2, c:c + 1])\
                        .then_inc(s_exp_done, 1)
                for c in range(DC):
                    act.wait_ge(s_am_done, c + 1)
                    nc.scalar.activation(lru_am[:, c, 1, :], lru_am[:, c, 1, :], ACT.Sqrt, scale=-1.0)\
                        .then_inc(s_mult_done, 1)
                for c in range(DC):
                    act.wait_ge(s_lru_val, c + 1)
                    nc.scalar.activation(lru_hl[:, c, 0, :], gelu[:, c, :], ACT.Copy).then_inc(s_lru_high, 1)

            def post(i):
                y = y_ffn if i == 3 else y_acc
                last = [group("o", l=i, ki=len(KINDS) - 1, m=m) if i < DEPTH else group(("o2", "down")[i - DEPTH], m=m)
                        for m in range(2)]
                for g in last:
                    for done_tile in group_drained(g):
                        act.wait_ge(*done_tile)
                if i == 2:
                    act.dma_start(x_res[:, :, :], x_spill).then_inc(s_x_back, 16)
                for t in range(TT):
                    link(nc.scalar.activation(probs[:, 0:2, :].rearrange("p a s -> p (a s)"), y[:, t, :],
                                              ACT.Square, accum_out=stat[:, 20 + t:21 + t]))
                link(nc.scalar.activation(stat[:, 24:28], stat[:, 20:24], ACT.Ln, bias=eps[:, 0:1], scale=1.0 / D))
                nc.scalar.activation(stat[:, 28:32], stat[:, 24:28], ACT.Exp, scale=-0.5).then_inc(s_y_scale, 1)

            started = False
            for st in STEPS:
                if st[0] == "block":
                    if not started:
                        high(0); high(1)
                        started = True
                    high(st[1] + 2)
                elif st[0] == "drain":
                    drain(st[1])
                elif st[0] == "norm":
                    norm(st[1])
                elif st[0] == "forget":
                    forget(st[1])
                elif st[0] == "rope":
                    rope(st[1])
                elif st[0] == "att":
                    _, l, kind, n = st
                    if n < 16:
                        soften(l, kind, n)
                    if 1 <= n <= 16:
                        turned(l, kind, n - 1)
                    if n >= 2 and (n - 2) % 4 == 3:
                        heads(l, kind, (n - 2) // 4)
                elif st[0] == "spill":
                    act.dma_start(x_spill, x_res[:, :, :]).then_inc(s_spilled, 16)
                    act.dma_start(wg, w_gates).then_inc(s_wg_in, 16)
                elif st[0] == "lru":
                    lru()
                elif st[0] == "angles":
                    act.wait_ge(s_ang_ready, 1)
                    nc.scalar.activation(rope_2[:, :, :, :], red[:, :, :, :], ACT.Sin).then_inc(s_sin_done, 1)
                elif st[0] == "mixsplit":
                    for m in range(2):
                        for done_tile in group_drained(group("mix", m=m, which=1)):
                            act.wait_ge(*done_tile)
                    for c in range(DC):
                        nc.scalar.activation(act_hl[:, c, 0, :], mix[:, c, :], ACT.Copy).then_inc(s_mix_high, 1)
                elif st[0] == "post":
                    post(st[1])

        @block.vector
        def _(dve):
            step = [0]

            def link(ins):
                step[0] += 1
                ins.then_inc(s_dve_step, 1)
                dve.wait_ge(s_dve_step, step[0])

            def setup():
                link(nc.vector.memset(ones[:, :], 1.0))
                link(nc.vector.memset(ck[:, :].bitcast(f32), 0.0))
                link(nc.vector.memset(eps[:, :], EPS))
                dve.wait_ge(s_consts, 16 * len(CONSTS))
                link(nc.vector.tensor_copy(sel_r[:, :, :], sel[:, :].unsqueeze(2).broadcast_to([P, 8, P])))
                for l in range(DEPTH):
                    link(nc.vector.tensor_scalar(sub_g[:, l:l + 1], sub_g[:, l:l + 1], 1.0 - LAM_INIT[l], None, ALU.mult))
                nc.vector.memset(xpad0[:, :], 0.0).then_inc(s_setup, 1)
                dve.wait_ge(s_setup, 1)

            def norm(i):
                dve.wait_ge(s_h_scale, i + 1)
                for t in range(TT):
                    nc.vector.tensor_scalar(y_acc[:, t, :], x_res[:, t, :], stat[:, 8 + t:9 + t], None, ALU.mult)\
                        .then_inc(s_h_rows, 1)
                for c in range(DC):
                    dve.wait_ge(s_norm_high, i * DC + c + 1)
                    nc.vector.scalar_tensor_tensor(
                        out=act_hl[:, c, 1, :], in0=bank[4 + c % 4][:, :], scalar=g_pre[:, i, c:c + 1],
                        in1=act_hl[:, c, 0, :].bitcast(f32), op0=ALU.mult, op1=ALU.subtract)\
                        .then_inc(freed(("norm", i, c)), 1)

            def forget(l):
                link(nc.vector.tensor_copy(wff_hl[:, 0], wff[:, l]))
                nc.vector.tensor_tensor(wff_hl[:, 1], wff[:, l], wff_hl[:, 0].bitcast(f32), ALU.subtract)\
                    .then_inc(s_ff_split, 1)
                prod = y_tmp[:, 0:2 * HD].rearrange("p (a d) -> p a d", a=2)
                link(nc.vector.tensor_tensor(prod, lv[:, l, 0::2, :], lv[:, l, 1::2, :], ALU.mult))
                nc.vector.tensor_reduce(lam[:, 0:2], prod, AX.X, ALU.add).then_inc(s_lam_dots, 1)
                dve.wait_ge(*full(("ff", l)))
                ps = bank_of(("ff", l))
                nc.vector.tensor_tensor(ffs[:, 0], ps[:, 0:TT * 8].rearrange("p (t h) -> p t h", h=8),
                                        fb[:, l, :].unsqueeze(1).broadcast_to([P, TT, 8]), ALU.add)\
                    .then_inc(freed(("ff", l)), 1)
                dve.wait_ge(s_ff_log, l + 1)
                dve.wait_ge(*drained(("ff", l)))
                nc.vector.scalar_tensor_tensor(out=ffs[:, 2], in0=ffs[:, 0], scalar=0.0, in1=ffs[:, 1],
                                               op0=ALU.min, op1=ALU.subtract).then_inc(s_ff_keep, 1)
                dve.wait_ge(s_lam_exp, l + 1)
                link(nc.vector.tensor_tensor(lam[:, 5:6], lam[:, 3:4], lam[:, 2:3], ALU.subtract))
                link(nc.vector.tensor_scalar(lam[:, 4:5], lam[:, 5:6], -LAM_INIT[l], None, ALU.add))
                dve.wait_ge(*full(("ffT", l)))
                ps = bank_of(("ffT", l))
                link(nc.vector.tensor_tensor_scan(ckf[0:8, :], ones[0:8, 0:1].broadcast_to([8, S]), ps[0:8, :],
                                                  0.0, ALU.mult, ALU.subtract))
                link(nc.vector.tensor_copy(ck[0:8, :], ckf[0:8, :]))
                nc.vector.tensor_tensor(ck[32:40, :], ckf[0:8, :], ck[0:8, :].bitcast(f32), ALU.subtract)\
                    .then_inc(freed(("ffT", l)), 1)

            def drain(gi):
                g = GROUPS[gi]
                tag = g["tag"]
                if tag not in ("o", "mix", "ffn", "down"):
                    return
                for j in range(4):
                    if tag == "ffn" and j < 2:
                        continue
                    dve.wait_ge(*tile_full(gi, j))
                    ps = bank[j]
                    done = freed(("dense", gi, j))
                    if tag == "o":
                        dst = y_acc[:, j, g["m"] * COLS:(g["m"] + 1) * COLS]
                        if g["ki"] == 0:
                            nc.vector.tensor_copy(dst, ps[:, :]).then_inc(done, 1)
                        else:
                            dve.wait_ge(*drained(("dense", group("o", l=g["l"], ki=g["ki"] - 1, m=g["m"])["index"], j)))
                            nc.vector.tensor_tensor(dst, ps[:, :], dst, ALU.add).then_inc(done, 1)
                    elif tag == "down":
                        nc.vector.tensor_copy(y_ffn[:, j, g["m"] * COLS:(g["m"] + 1) * COLS], ps[:, :]).then_inc(done, 1)
                    elif tag == "mix":
                        dve.wait_ge(*drained(("dense", gi - 1, j)))
                        dst = mix[:, 4 * g["m"] + j, :]
                        if g["which"] == 0:
                            if j == 0:
                                dve.wait_ge(s_spilled, 16)
                            nc.vector.tensor_tensor(dst, ps[:, :], sig[:, j, :], ALU.mult).then_inc(done, 1)
                        else:
                            link(nc.vector.tensor_tensor(y_tmp[:, :], ps[:, :], sig[:, j, :], ALU.mult))
                            nc.vector.tensor_tensor(dst, dst, y_tmp[:, :], ALU.add).then_inc(done, 1)
                            dve.wait_ge(*drained(("dense", gi, j)))
                    elif tag == "ffn":
                        n = 2 * g["m"] + j - 2
                        dve.wait_ge(*drained(("dense", gi, j - 2)))
                        if n - 1 > 0:
                            dve.wait_ge(s_hid_low, n - 1)
                        link(nc.vector.tensor_tensor(probs[:, j, :], ps[:, :], probs[:, j - 2, :], ALU.mult))
                        dve.sem_inc(s_hid_val, 1)
                        dve.sem_inc(done, 1)
                        dve.wait_ge(s_hid_high, n + 1)
                        nc.vector.tensor_tensor(hid_hl[:, n, 1, :], probs[:, j, :], hid_hl[:, n, 0, :].bitcast(f32),
                                                ALU.subtract).then_inc(s_hid_low, 1)

            def rope(gi, nth):
                g = GROUPS[gi]
                for t in range(TT):
                    dve.wait_ge(*drained(("dense", gi, t)))
                if g["tag"] in ("q2", "k2"):
                    dve.wait_ge(s_sin_done, 1)
                F, table = (2 * HD, rope_2) if g["tag"] in ("q2", "k2") else (HD, rope_1)
                nh, half = COLS // F, table.shape[3]
                rows = tok_tmp.rearrange("p t (h f) -> p t h f", f=F)
                r1, r2 = rows[:, :, :, 0:half], rows[:, :, :, half:2 * half]
                c = table[:, 0].unsqueeze(2).broadcast_to([P, TT, nh, half])
                s = table[:, 1].unsqueeze(2).broadcast_to([P, TT, nh, half])
                tmp = y_tok[:, :, :, :].rearrange("p a t f -> p (a t f)").rearrange(
                    "p (k t h f) -> p k t h f", k=4, t=TT, h=nh)
                link(nc.vector.tensor_tensor(tmp[:, 0], r1, c, ALU.mult))
                link(nc.vector.tensor_tensor(tmp[:, 1], r2, s, ALU.mult))
                link(nc.vector.tensor_tensor(tmp[:, 2], r2, c, ALU.mult))
                link(nc.vector.tensor_tensor(tmp[:, 3], r1, s, ALU.mult))
                link(nc.vector.tensor_tensor(r1, tmp[:, 0], tmp[:, 1], ALU.subtract))
                nc.vector.tensor_tensor(r2, tmp[:, 2], tmp[:, 3], ALU.add).then_inc(s_roped, 1)
                dve.wait_ge(s_roped, nth)

            def soften(l, kind, n):
                par, i = n % 2, n % 4
                if kind == "sb":
                    for a in range(2):
                        _, nb = geometry(kind, a, i)
                        row = probs[:, p_slot(kind, n, a), 0:nb * P]
                        back = row[:, ::-1]
                        dve.wait_ge(*full(("S", l, kind, n, a)))
                        ps = bank_of(("S", l, kind, n, a))
                        dve.wait_ge(s_abs_log, MARKS["abs_log", (l, kind, n, a)])
                        link(nc.vector.scalar_tensor_tensor(out=row, in0=ps[:, 0:nb * P], scalar=0.0, in1=row,
                                                            op0=ALU.max, op1=ALU.add))
                        link(nc.vector.tensor_tensor_scan(back, ones[:, 0:1].broadcast_to([P, nb * P]), back,
                                                          0.0, ALU.mult, ALU.add))
                        nc.vector.tensor_tensor(row, ps[:, 0:nb * P], row, ALU.subtract)\
                            .then_inc(freed(("S", l, kind, n, a)), 1)
                    return
                for a in unit_maps(kind):
                    _, nb = geometry(kind, a, i)
                    dve.wait_ge(*full(("S", l, kind, n, a)))
                    ps = bank_of(("S", l, kind, n, a))
                    if kind == "dil":
                        link(nc.vector.tensor_reduce(stat[:, 32 + a:33 + a], ps[:, 0:nb * P], AX.X, ALU.max))
                    else:
                        nc.vector.tensor_reduce(nmax[:, par, a:a + 1], ps[:, 0:nb * P], AX.X, ALU.max, negate=True)\
                            .then_inc(s_rows_max, 1)
                if kind == "dil":
                    nc.vector.tensor_reduce(nmax[:, par, 0:1], stat[:, 32:35], AX.X, ALU.max, negate=True)\
                        .then_inc(s_rows_max, 1)
                for a in unit_maps(kind):
                    dve.wait_ge(*drained(("S", l, kind, n, a)))
                if kind == "dil":
                    link(nc.vector.tensor_reduce(stat[:, 36:37], sums[:, par, 0:3], AX.X, ALU.add))
                    link(nc.vector.reciprocal(rinv[:, par, 0:1], stat[:, 36:37]))
                    return
                link(nc.vector.reciprocal(rinv[:, par, 0:2], sums[:, par, 0:2]))
                if kind == "diff":
                    _, nb = geometry(kind, 0, i)
                    r0, r1 = (probs[:, p_slot(kind, n, a), 0:nb * P] for a in range(2))
                    link(nc.vector.tensor_tensor(rinv[:, par, 1:2], rinv[:, par, 1:2], lam[:, 4:5], ALU.mult))
                    link(nc.vector.tensor_scalar(r0, r0, rinv[:, par, 0:1], None, ALU.mult))
                    nc.vector.scalar_tensor_tensor(out=r0, in0=r1, scalar=rinv[:, par, 1:2], in1=r0,
                                                   op0=ALU.mult, op1=ALU.add).then_inc(s_soft, 1)

            def turned(l, kind, n):
                for a in value_maps(kind):
                    if a % 2 == 1:
                        copy_turned(dve, nc.vector, l, kind, n, a)
                p, i, par = n // 4, n % 4, n % 2
                dve.wait_ge(s_pv_done, USE["map", l, kind, n, value_maps(kind)[-1]] + 1)
                if i == 0 and p >= 2:
                    dve.wait_ge(*full(("Y", l, kind, p - 2)))
                dst = y_tok[:, p % 2, i, :]
                o = bank[BO]
                done = freed(("O", l, kind, n))
                if kind == "diff":
                    dve.wait_ge(s_rms, MARKS["rms", (l, kind, n)])
                    nc.vector.tensor_scalar(dst, o[:, 0:P], stat[:, 18 + par:19 + par], None, ALU.mult).then_inc(done, 1)
                elif kind == "sb":
                    nc.vector.tensor_copy(dst, o[:, 0:P]).then_inc(done, 1)
                elif kind == "dil":
                    nc.vector.tensor_scalar(dst, o[:, 0:P], rinv[:, par, 0:1], None, ALU.mult).then_inc(done, 1)
                else:
                    nc.vector.tensor_scalar(dst[:, 0:HD], o[:, 0:HD], rinv[:, par, 0:1], None, ALU.mult)
                    nc.vector.tensor_scalar(dst[:, HD:P], o[:, HD:P], rinv[:, par, 1:2], None, ALU.mult).then_inc(done, 1)

            def heads(l, kind, p):
                dve.wait_ge(*full(("Y", l, kind, p)))
                ps = bank_of(("Y", l, kind, p))
                if kind == "dil":
                    dve.wait_ge(s_y_high, MARKS["y_high", (l, kind, p)])
                    nc.vector.tensor_tensor(y_hl[:, p, 1, :], ps[:, :], y_hl[:, p, 0, :].bitcast(f32), ALU.subtract)\
                        .then_inc(freed(("Y", l, kind, p)), 1)
                    return
                if p == 0:
                    for done_tile in group_drained(group("g", l=l, kind=kind)):
                        dve.wait_ge(*done_tile)
                scalar = sub_g[:, l:l + 1] if kind == "diff" else 1.0
                nc.vector.scalar_tensor_tensor(out=y_tmp[:, :], in0=ps[:, :], scalar=scalar, in1=gate[:, p, :],
                                               op0=ALU.mult, op1=ALU.mult).then_inc(freed(("Y", l, kind, p)), 1)
                dve.wait_ge(s_y_high, MARKS["y_high", (l, kind, p)])
                dve.wait_ge(*drained(("Y", l, kind, p)))
                nc.vector.tensor_tensor(y_hl[:, p, 1, :], y_tmp[:, :], y_hl[:, p, 0, :].bitcast(f32), ALU.subtract)\
                    .then_inc(s_y_low, 1)
                dve.wait_ge(s_y_low, MARKS["y_low", (l, kind, p)])

            def lru():
                for m in range(2):
                    for done_tile in group_drained(group("xr", m=m)):
                        dve.wait_ge(*done_tile)
                dve.wait_ge(s_lam_log, 1)
                link(nc.vector.tensor_scalar(lam8[:, 2], lam8[:, 0], -1.0, 0.0, ALU.mult, ALU.max))
                link(nc.vector.tensor_tensor(lam8[:, 2], lam8[:, 2], lam8[:, 1], ALU.add))
                nc.vector.tensor_scalar(lam8[:, 2], lam8[:, 2], -8.0, None, ALU.mult).then_inc(s_lam8_ready, 1)
                link(nc.vector.memset(xpad[:, :, 0:PAD], 0.0))
                for c in range(DC):
                    dst = xc[:, c, :]
                    link(nc.vector.tensor_scalar(dst, xpad[:, c, 1:1 + S], cw[:, c, 0:1], cb[:, c:c + 1], ALU.mult, ALU.add))
                    for j in range(1, 4):
                        op = nc.vector.scalar_tensor_tensor(out=dst, in0=xpad[:, c, 1 + j:1 + j + S], scalar=cw[:, c, j:j + 1],
                                                            in1=dst, op0=ALU.mult, op1=ALU.add)
                        if j < 3:
                            link(op)
                    op.then_inc(s_conv_done, 1)
                    if c >= 1:
                        inputs(c - 1)
                inputs(DC - 1)
                for m in range(2):
                    for done_tile in group_drained(group("gr", m=m)):
                        dve.wait_ge(*done_tile)
                dve.wait_ge(s_ix_done, DC)
                for c in range(DC):
                    dve.wait_ge(s_exp_done, c + 1)
                    link(nc.vector.tensor_tensor(probs_t[:, 0, :], lru_am[:, c, 0, :], lru_am[:, c, 0, :], ALU.mult))
                    nc.vector.scalar_tensor_tensor(out=lru_am[:, c, 1, :], in0=probs_t[:, 0, :], scalar=1.0,
                                                   in1=lru_am[:, c, 1, :], op0=ALU.add, op1=ALU.mult).then_inc(s_am_done, 1)
                    dve.wait_ge(s_am_done, c + 1)
                for c in range(DC):
                    dve.wait_ge(s_mult_done, c + 1)
                    link(nc.vector.memset(lru_am[:, c, 1, 0:1], 1.0))
                    link(nc.vector.tensor_tensor(xc[:, c, :], lru_am[:, c, 1, :], xc[:, c, :], ALU.mult))
                    link(nc.vector.tensor_tensor_scan(xpad[:, c, PAD:], lru_am[:, c, 0, :], xc[:, c, :], 0.0, ALU.mult, ALU.add))
                    nc.vector.tensor_tensor(gelu[:, c, :], xpad[:, c, PAD:], gelu[:, c, :], ALU.mult).then_inc(s_lru_val, 1)
                for c in range(DC):
                    dve.wait_ge(s_lru_high, c + 1)
                    dve.wait_ge(s_lru_val, c + 1)
                    nc.vector.tensor_tensor(lru_hl[:, c, 1, :], gelu[:, c, :], lru_hl[:, c, 0, :].bitcast(f32), ALU.subtract)\
                        .then_inc(s_lru_low, 1)

            def inputs(c):
                dve.wait_ge(*drained(("i", c)))
                nc.vector.tensor_tensor(xc[:, c, :], probs[:, 4 + c % 2, :], xc[:, c, :], ALU.mult).then_inc(s_ix_done, 1)

            def angles():
                link(nc.vector.tensor_copy(posf[:, :], posi[:, :]))
                hf = ROT2 // 2
                link(nc.vector.tensor_tensor(ang[:, :, :], posf[:, :].unsqueeze(2).broadcast_to([P, TT, hf]),
                                             invf[:, :].unsqueeze(1).broadcast_to([P, TT, hf]), ALU.mult))
                big = 1.5 * 2.0 ** 23
                hi, mid = 6.28125, 0.00193500518798828125
                low = 2 * math.pi - hi - mid
                for s, (off, add) in enumerate(((0.25, math.pi / 2), (0.0, 0.0))):
                    link(nc.vector.tensor_scalar(turns[:, s], ang[:, :, :], 1 / (2 * math.pi), off, ALU.mult, ALU.add))
                    link(nc.vector.tensor_scalar(turns[:, s], turns[:, s], big, None, ALU.add))
                    link(nc.vector.tensor_scalar(turns[:, s], turns[:, s], -big, None, ALU.add))
                    link(nc.vector.scalar_tensor_tensor(out=red[:, s], in0=turns[:, s], scalar=-hi, in1=ang[:, :, :],
                                                        op0=ALU.mult, op1=ALU.add))
                    for part in (mid, low):
                        link(nc.vector.scalar_tensor_tensor(out=red[:, s], in0=turns[:, s], scalar=-part, in1=red[:, s],
                                                            op0=ALU.mult, op1=ALU.add))
                    link(nc.vector.tensor_scalar(red[:, s], red[:, s], add, None, ALU.add))
                PI = 3.1415925
                nc.vector.tensor_scalar(red[:, :, :, :], red[:, :, :, :], PI, -PI, ALU.min, ALU.max).then_inc(s_ang_ready, 1)

            def post(i):
                y = y_ffn if i == 3 else y_acc
                dve.wait_ge(s_y_scale, i + 1)
                dve.wait_ge(s_gain_in, 16 * (i + 1))
                if i == 2:
                    dve.wait_ge(s_x_back, 16)
                for t in range(TT):
                    link(nc.vector.scalar_tensor_tensor(out=y[:, t, :], in0=y[:, t, :], scalar=stat[:, 28 + t:29 + t],
                                                        in1=g_post[:, :], op0=ALU.mult, op1=ALU.mult))
                    nc.vector.tensor_tensor(x_res[:, t, :], x_res[:, t, :], y[:, t, :], ALU.add).then_inc(s_x_new, 1)

            setup()
            ropes = 0
            for st in STEPS:
                if st[0] == "drain":
                    drain(st[1])
                elif st[0] == "norm":
                    norm(st[1])
                elif st[0] == "forget":
                    forget(st[1])
                elif st[0] == "rope":
                    ropes += 1
                    rope(st[1], ropes)
                elif st[0] == "att":
                    _, l, kind, n = st
                    if n < 16:
                        soften(l, kind, n)
                    if 1 <= n <= 16:
                        turned(l, kind, n - 1)
                    if n >= 2 and (n - 2) % 4 == 3:
                        heads(l, kind, (n - 2) // 4)
                elif st[0] == "lru":
                    lru()
                elif st[0] == "angles":
                    angles()
                elif st[0] == "mixsplit":
                    for c in range(DC):
                        dve.wait_ge(s_mix_high, c + 1)
                        nc.vector.tensor_tensor(act_hl[:, c, 1, :], mix[:, c, :], act_hl[:, c, 0, :].bitcast(f32),
                                                ALU.subtract).then_inc(s_mix_low, 1)
                elif st[0] == "post":
                    post(st[1])


def kernel(**inputs):
    import concourse.bacc as bacc
    import ml_dtypes
    from concourse.bass_utils import run_bass_kernel_spmd

    a = {k: np.asarray(v) for k, v in inputs.items()}
    f = np.float32

    def by_chunk(v):
        v = v.reshape(v.shape[:-1] + (-1, P))
        return np.ascontiguousarray(np.moveaxis(v, -1, 0))

    def columns(g):
        tag, w1, w2 = g["tag"], a["w_in"], a["w_in_2"][0]
        if tag in ("q", "k", "v", "g"):
            at = 4 * COLS * ("diff", "sb", "fox").index(g["kind"]) + COLS * "qkvg".index(tag)
            return w1[g["l"]][:, at:at + COLS]
        if tag == "o":
            r = COLS * ("diff", "sb", "fox").index(g["kind"])
            return a["w_out"][g["l"]][r:r + COLS, g["m"] * COLS:(g["m"] + 1) * COLS]
        if tag in ("q2", "k2", "v2"):
            at = 2 * D + G2 * COLS * ("q2", "k2", "v2").index(tag) + COLS * g["g"]
            return w2[:, at:at + COLS]
        if tag == "ffn":
            h = slice(g["m"] * COLS // 2, (g["m"] + 1) * COLS // 2)
            return np.concatenate([a["w_ffn_gate_2"][0][:, h], a["w_ffn_up_2"][0][:, h]], axis=1)
        c = slice(g["m"] * COLS, (g["m"] + 1) * COLS)
        if tag == "xr":
            return w2[:, c]
        if tag == "gr":
            return w2[:, D:2 * D][:, c]
        if tag == "gate":
            at = 2 * D + 3 * G2 * COLS + D * g["which"]
            return w2[:, at:at + D][:, c]
        if tag == "mix":
            return (a["w_attn_proj_2"] if g["which"] else a["w_lru_proj_2"])[0][:, c]
        if tag == "o2":
            return a["w_out_2"][0][:, c]
        return a["w_ffn_down_2"][0][:, c]

    stream = np.empty((NB, P, BC, COLS), f)
    for b, (gi, k) in enumerate(BLOCKS):
        w = columns(GROUPS[gi])[k * BC * P:(k + 1) * BC * P]
        stream[b] = w.reshape(BC, P, COLS).transpose(1, 0, 2)

    q, k = np.arange(P)[:, None], np.arange(P)[None, :]
    seen = {"causal": k <= q, "strict": k < q, "chunk": k // 64 <= q // 64, "prev": k >= q,
            "mod4d": (k <= q) & ((q - k) % 4 == 0), "mod4": (q - k) % 4 == 0,
            "mod16d": (k <= q) & ((q - k) % 16 == 0), "mod16": (q - k) % 16 == 0}
    masks = np.stack([np.where(seen[m], 0.0, NEG) for m in MASKS] + [np.eye(P)]).astype(ml_dtypes.bfloat16)
    sel = np.zeros((P, 8), f)
    sel[np.arange(8), np.arange(8)] = 1
    sel[32 + np.arange(8), np.arange(8)] = 1
    freq1 = f(500000.0) ** (-np.arange(0, ROT1, 2, dtype=f) / f(ROT1))
    freq2 = f(500000.0) ** (-np.arange(0, ROT2, 2, dtype=f) / f(ROT2))
    angle = np.arange(S, dtype=f)[:, None] * freq1[None]
    rope1 = np.stack([np.cos(angle), np.sin(angle)]).astype(f).reshape(2, TT, P, ROT1 // 2).transpose(2, 0, 1, 3)

    w_gates = np.zeros((P, 2, DC, P), f)
    for w, name in enumerate(("w_rg_2", "w_ig_2")):
        blocks = a[name][0].reshape(DC, 2, 64, 64)
        for h in range(2):
            w_gates[64 * h:64 * h + 64, w, :, 64 * h:64 * h + 64] = blocks[:, h].transpose(1, 0, 2)

    given = {
        "x": a["x"],
        "wstream": stream.reshape(NB, P, BC * COLS),
        "w_ff": a["w_in"][:, :, 12 * COLS:].reshape(DEPTH, DC, P, 8).transpose(2, 0, 1, 3),
        "f_bias": np.broadcast_to(a["forget_bias"][None], (P, DEPTH, 8)),
        "lam_vec": np.broadcast_to(a["diff_lambda"][None], (P, DEPTH, 4, HD)),
        "subln": a["diff_subln"].T,
        "gains": by_chunk(np.concatenate([a["pre_norm"], a["pre_mix_norm_2"], a["pre_ffn_norm_2"]])),
        "post_gains": np.concatenate([a["post_norm"], a["post_mix_norm_2"], a["post_ffn_norm_2"]]),
        "masks": masks.transpose(1, 0, 2),
        "ident_in": np.eye(P, dtype=f),
        "sel_in": sel,
        "rope1": rope1,
        "positions": a["positions_2"].reshape(TT, P).T,
        "inv_freq": np.broadcast_to(freq2[None], (P, ROT2 // 2)),
        "conv_w": by_chunk(a["conv_w_2"][0]).transpose(0, 2, 1),
        "conv_b": by_chunk(a["conv_b_2"][0]),
        "w_gates": w_gates.reshape(P, 2 * DC, P),
        "b_gates": by_chunk(np.concatenate([a["b_rg_2"], a["b_ig_2"]])),
        "lru_lambda": by_chunk(a["lru_lambda_2"][0]),
    }
    nc = bacc.Bacc("TRN2", target_bir_lowering=False, num_devices=1)
    args = {}
    for name, v in given.items():
        given[name] = v = np.ascontiguousarray(v)
        args[name] = nc.dram_tensor(name, v.shape, mybir.dt.from_np(v.dtype), kind="ExternalInput").ap()
    args["x_spill"] = nc.dram_tensor("x_spill", (P, TT, D), mybir.dt.float32, kind="Internal").ap()
    args["out"] = nc.dram_tensor("out", (1, S, D), mybir.dt.float32, kind="ExternalOutput").ap()
    build(nc, **args)
    return run_bass_kernel_spmd(nc, [given], core_ids=[0]).results[0]["out"]
```

```python
import math

import numpy as np

import concourse.bass as bass
from concourse import mybir

S, D, P = 512, 1024, 128
TT, DC = S // P, D // P
DEPTH, HD = 2, 64
KINDS = ("diff", "sb", "fox")
ROT1, ROT2 = 16, 32
H2, G2 = 4, 3
D_FF = 2816
FC = D_FF // P
NEG = -1e30
EPS = 1e-6
BC = 2
COLS = 512
RING = 4
LAM_INIT = [0.8 - 0.6 * math.exp(-0.3 * l) for l in range(DEPTH)]
HEADS_AT = (8, 13, 17, 18)
ATT_STEPS = 19
NORM_CHUNKS = (range(DC // 2), range(DC // 2, DC))
LRU_EARLY = 7
S0, S1, BT, BO = 4, 5, 6, 7
MASKS = ("causal", "strict", "chunk", "prev", "mod4d", "mod4", "mod16d", "mod16")


def plan():
    groups, steps, blocks = [], [], []

    def dense(tag, rows, orient, **more):
        g = dict(tag=tag, n=rows // BC, orient=orient, index=len(groups), first=len(blocks), **more)
        groups.append(g)
        out = []
        for k in range(g["n"]):
            out.append(("block", len(blocks), len(groups) - 1, k, (0, 1, 2, 3)))
            blocks.append((len(groups) - 1, k))
        out.append(("drain", len(groups) - 1))
        return out

    def weave(dense_steps, others, early, first):
        dense_steps = [half for st in dense_steps
                       for half in ([st[:4] + ((0, 1),), st[:4] + ((2, 3),)] if st[0] == "block" else [st])]
        n = sum(st[0] == "block" for st in dense_steps)
        early *= 2
        due = [early * (i + 1) / first for i in range(first)]
        due += [early + (n - early) * (i + 1 - first) / (len(others) - first) for i in range(first, len(others))]
        out, rest, seen = [], list(dense_steps), 0
        for other, upto in zip(others, due):
            while rest and (seen < math.ceil(upto + 0.75) or rest[0][0] != "block"):
                seen += rest[0][0] == "block"
                out.append(rest.pop(0))
            out.append(other)
        return out + rest

    def tile_by_tile(dense_steps):
        *rest, one, two, drain = dense_steps
        return rest + [blk[:4] + ((j,),) for j in range(4) for blk in (one, two)] + [drain]

    def attention(l, kind):
        return [("att", l, kind, n, part) for n in range(ATT_STEPS) for part in range(2)]

    def project(tag, l, ki):
        turn = KINDS[ki] == "diff" and tag in "qk"
        out = dense(tag, DC, "tok" if turn or tag == "v" else "feat", l=l, kind=KINDS[ki], ki=ki)
        return out + ([("rope", len(groups) - 1)] if turn else [])

    def output(l, ki):
        return [st for m in range(2) for st in dense("o", 4, "tok", l=l, kind=KINDS[ki], ki=ki, m=m)]

    for l in range(DEPTH):
        steps.append(("norm", l))
        for tag in "qkv":
            steps += project(tag, l, 0)
            if tag == "q":
                steps.append(("forget", l))
        for ki in range(len(KINDS)):
            between = (output(l, ki - 1) if ki else []) + project("g", l, ki)
            early = sum(st[0] == "block" for st in between)
            if ki + 1 < len(KINDS):
                between += project("q", l, ki + 1) + project("k", l, ki + 1)
            steps += weave(between, attention(l, KINDS[ki]), early, 2 * HEADS_AT[0])
            if ki + 1 < len(KINDS):
                steps += project("v", l, ki + 1)
        steps += tile_by_tile(output(l, len(KINDS) - 1))
        steps.append(("post", l))
    steps.append(("norm", 2))
    steps.append(("spill",))
    for m in range(2):
        steps += dense("xr", DC, "feat", m=m)
    between = []
    for tag in ("gr", "gate"):
        for m in range(2):
            between += dense(tag, DC, "feat", m=m, which=0)
    lru = [("lru", part, c) for part in ("decide", "decay", "scale", "scan") for c in range(DC)]
    steps += weave(between, lru, LRU_EARLY, DC)
    for m in range(2):
        steps += dense("mix", DC, "feat", m=m, which=0)
    steps.append(("angles",))
    for g in range(G2):
        for tag in ("q2", "k2"):
            steps += dense(tag, DC, "tok", g=g)
            steps += [("rope", len(groups) - 1)]
        steps += dense("v2", DC, "tok", g=g)
    steps += attention(2, "dil")
    for m in range(2):
        steps += dense("gate", DC, "feat", m=m, which=1)
    for m in range(2):
        steps += dense("mix", 4, "feat", m=m, which=1)
        steps.append(("mixsplit", m))
    steps += dense("o2", DC, "tok", m=0) + tile_by_tile(dense("o2", DC, "tok", m=1))
    steps.append(("post", 2))
    steps.append(("norm", 3))
    for m in range(FC // 2):
        steps += dense("ffn", DC, "feat", m=m)
    steps += dense("down", FC, "tok", m=0) + tile_by_tile(dense("down", FC, "tok", m=1))
    steps.append(("post", 3))

    late, pending = [], None
    for st in steps:
        late.append(st)
        if st[0] == "rope":
            pending = ("ropeturn", st[1])
        elif st[0] == "norm":
            late.append(("normturn", st[1], 0))
            pending = ("normturn", st[1], 1)
        elif pending is not None and st[0] == "block" and st[4][-1] == 3:
            late.append(pending)
            pending = None
    steps = late

    used, full, use = [0] * 8, [0] * 8, {}
    maps = 0

    def take(key, bank, signal=True):
        use[key] = (bank, used[bank], full[bank] + 1 if signal else None)
        used[bank] += 1
        full[bank] += 1 if signal else 0

    marks, count = {}, {}

    def mark(name, key):
        count[name] = count.get(name, 0) + 1
        marks[name, key] = count[name]

    for st in steps:
        if st[0] == "drain":
            for j in range(4):
                take(("dense", st[1], j), j, signal=j < 3)
        elif st[0] == "normturn":
            for c in NORM_CHUNKS[st[2]]:
                take(("norm", st[1], c), 4 + c % 4)
        elif st[0] == "forget":
            take(("ff", st[1]), S0)
        elif st[0] == "ropeturn":
            for j in range(4):
                take(("rope", st[1], j), 4 + j)
        elif st[:2] == ("lru", "decide"):
            take(("r", st[2]), 4 + 2 * (st[2] % 2))
            take(("i", st[2]), 5 + 2 * (st[2] % 2))
        elif st[0] == "att":
            _, l, kind, n, part = st
            turn, value = n - 1, n - 2
            if 0 <= turn < 16:
                for a in value_maps(kind):
                    if (a > 0) == part:
                        take(("T", l, kind, turn, a), (BT, 0, 1)[a] if kind == "dil" else BT)
            if n < 16 and part == 0:
                for a in unit_maps(kind):
                    take(("S", l, kind, n, a), (S0, S1, 3)[a])
                if kind in ("diff", "fox"):
                    for a in range(2):
                        mark("rows_max", (l, kind, n, a))
                if kind == "dil":
                    mark("rows_max", (l, kind, n, 0))
                if kind == "sb":
                    for a in range(2):
                        mark("abs_log", (l, kind, n, a))
                        mark("soft", (l, kind, n, a))
                if kind == "diff":
                    mark("soft", (l, kind, n, 0))
            if 0 <= value < 16 and part == 0:
                for a in value_maps(kind):
                    use[("map", l, kind, value, a)] = maps
                    maps += 1
                take(("O", l, kind, value), BO, signal=False)
                if kind == "diff":
                    mark("rms", (l, kind, value))
            if n in HEADS_AT and part == 1:
                p = HEADS_AT.index(n)
                take(("Y", l, kind, p), BT)
                mark("y_high", (l, kind, p))
                mark("y_low", (l, kind, p))
    return steps, groups, blocks, use, marks


def unit_maps(kind):
    return range(3 if kind == "dil" else 2)


def value_maps(kind):
    return {"diff": range(1), "dil": range(3)}.get(kind, range(2))


STEPS, GROUPS, BLOCKS, USE, MARKS = plan()
NB = len(BLOCKS)


def build(nc, x, wstream, w_ff, f_bias, lam_vec, subln, gains, post_gains, masks, ident_in, sel_in, rope1, positions,
          inv_freq, conv_w, conv_b, w_gates, b_gates, lru_lambda, x_spill, out):
    f32, f32r, bf16, i32 = mybir.dt.float32, mybir.dt.float32r, mybir.dt.bfloat16, mybir.dt.int32
    ALU, ACT, AX = mybir.AluOpType, mybir.ActivationFunctionType, mybir.AxisListType
    cursor = [(nc.sbuf_base + 63) // 64 * 64]

    def at(name, shape, dt, offset=None):
        size = int(np.prod(shape[1:])) * mybir.dt.size(dt)
        if offset is None:
            offset = cursor[0]
            cursor[0] += (size + 63) // 64 * 64
        return nc.alloc_sbuf_tensor_at(name, list(shape), dt, offset=offset)

    x_res = at("x_res", [P, TT, D], f32)
    mix = x_res[:, :, :].rearrange("p t (a s) -> p (t a) s", s=S)
    act_at = cursor[0]
    act_hl = at("act_hl", [P, DC, 2, S], f32r)
    y_ffn = at("y_ffn", [P, TT, D], f32, act_at)
    ring_at = cursor[0]
    w_hl = at("w_hl", [P, RING, 2, BC, COLS], f32r)
    w_raw = at("w_raw", [P, RING, 2, BC * COLS], f32, ring_at)[:, :, 1, :]
    probs = at("probs", [P, 9, S], f32)
    tok_tmp = probs[:, 0:4, :]
    sig = probs[:, 0:8, :]
    ff_in, ff_log = probs[0:8, 4, :], probs[0:8, 5, :]
    probs_t = probs[:, 6:9, :]
    y_tok = at("y_tok", [P, 2, TT, P], f32)
    diag = y_tok[:, 0]
    y_tmp = at("y_tmp", [P, S], f32)
    arena = cursor[0]
    y_hl = at("y_hl", [P, 4, 2, S], f32r)
    over = cursor[0]
    y_acc = at("y_acc", [P, TT, D], f32)
    gate = at("gate", [P, 4, S], f32)
    qT = at("qT", [P, 2, 4, S], f32)
    kT = at("kT", [P, 2, 4, S], f32)
    vv = at("vv", [P, TT, 4 * P], f32)
    sel_r = at("sel_r", [P, 8], f32r)
    ck = at("ck", [P, S], f32r)
    ckf = at("ckf", [P, S], f32)
    wff = at("wff", [P, DEPTH, DC, 8], f32)
    wff_hl = at("wff_hl", [P, 2, DC, 8], f32r)
    lv = at("lv", [P, DEPTH, 4, HD], f32)
    lru_am = at("lru_am", [P, DC, 2, S], f32, arena)
    lru_hl = at("lru_hl", [P, DC, 2, S], f32r, arena)
    PAD = 4
    xpad = at("xpad", [P, DC, PAD + S], f32, arena + 32768)
    xc = at("xc", [P, DC, S], f32, arena + 32768 + DC * (PAD + S) * 4)
    gelu = at("gelu", [P, DC, S], f32, arena + 49152 + DC * (PAD + S) * 4)
    q2 = at("q2", [P, G2 * H2, S], f32, over)
    k2 = at("k2", [P, G2 * H2, S], f32, over + 24576)
    v2 = at("v2", [P, TT, G2 * H2 * P], f32, over + 49152)
    hid_hl = at("hid_hl", [P, FC, 2, S], f32r, arena)
    cursor[0] = max(cursor[0], arena + FC * 2 * S * 4)
    mask_b = at("mask_b", [P, len(MASKS) + 1, P], bf16)
    ident = at("ident", [P, P], f32)
    sel = at("sel", [P, 8], f32)
    y_sq = at("y_sq", [P, P], f32)
    ones = at("ones", [P, 1], f32)
    eps = at("eps", [P, 1], f32)
    g_pre = at("g_pre", [P, 4, DC], f32)
    g_post = at("g_post", [P, D], f32)
    fb = at("fb", [8, DEPTH], f32)
    sub_g = at("sub_g", [P, DEPTH], f32)
    rope_1 = at("rope_1", [P, 2, TT, ROT1 // 2], f32)
    rope_2 = at("rope_2", [P, 2, TT, ROT2 // 2], f32)
    ang = at("ang", [P, TT, ROT2 // 2], f32)
    red = at("red", [P, 2, TT, ROT2 // 2], f32)
    turns = at("turns", [P, 2, TT, ROT2 // 2], f32)
    posi = at("posi", [P, TT], i32)
    posf = at("posf", [P, TT], f32)
    invf = at("invf", [P, ROT2 // 2], f32)
    cw = at("cw", [P, DC, 4], f32)
    cb = at("cb", [P, DC], f32)
    wg = probs[:, 0:4, :].rearrange("p a (b n) -> p (a b) n", n=P)
    bg = at("bg", [P, 2, DC], f32)
    lam8 = at("lam8", [P, 3, DC], f32)
    stat = at("stat", [P, 64], f32)
    sums = at("sums", [P, 2, 4], f32)
    nmax = at("nmax", [P, 2, 4], f32)
    rinv = at("rinv", [P, 4, 2], f32)
    lam = at("lam", [P, 8], f32)

    bank = [nc.alloc_psum_tensor(f"bank{i}", [P, S], f32) for i in range(8)]

    s_high_done = nc.alloc_semaphore("high_done")
    s_low_done = nc.alloc_semaphore("low_done")
    s_block_used = nc.alloc_semaphore("block_used")
    s_consts = nc.alloc_semaphore("consts")
    s_first = nc.alloc_semaphore("first")
    s_dve_step = nc.alloc_semaphore("dve_step")
    s_act_step = nc.alloc_semaphore("act_step")
    s_rows_max = nc.alloc_semaphore("rows_max")
    s_abs_log = nc.alloc_semaphore("abs_log")
    s_soft = nc.alloc_semaphore("soft")
    s_pv_done = nc.alloc_semaphore("pv_done")
    s_rms = nc.alloc_semaphore("rms")
    s_y_high = nc.alloc_semaphore("y_high")
    s_y_low = nc.alloc_semaphore("y_low")
    x_in = [nc.alloc_semaphore(f"x_in{t}") for t in range(TT)]
    s_x_new = nc.alloc_semaphore("x_new")
    s_h_scale = nc.alloc_semaphore("h_scale")
    s_h_rows = nc.alloc_semaphore("h_rows")
    s_norm_high = nc.alloc_semaphore("norm_high")
    s_gain_in = nc.alloc_semaphore("gain_in")
    s_roped = nc.alloc_semaphore("roped")
    s_ff_split = nc.alloc_semaphore("ff_split")
    s_ff_log = nc.alloc_semaphore("ff_log")
    s_ck_ready = nc.alloc_semaphore("ck_ready")
    s_lam_dots = nc.alloc_semaphore("lam_dots")
    s_lam_exp = nc.alloc_semaphore("lam_exp")
    s_spilled = nc.alloc_semaphore("spilled")
    s_wg_in = nc.alloc_semaphore("wg_in")
    s_conv_done = nc.alloc_semaphore("conv_done")
    s_ix_done = nc.alloc_semaphore("ix_done")
    s_exp_done = nc.alloc_semaphore("exp_done")
    s_am_done = nc.alloc_semaphore("am_done")
    s_mult_done = nc.alloc_semaphore("mult_done")
    s_lru_val = nc.alloc_semaphore("lru_val")
    s_lru_high = nc.alloc_semaphore("lru_high")
    s_lru_low = nc.alloc_semaphore("lru_low")
    s_lam_log = nc.alloc_semaphore("lam_log")
    s_lam8_ready = nc.alloc_semaphore("lam8_ready")
    s_ang_ready = nc.alloc_semaphore("ang_ready")
    s_sin_done = nc.alloc_semaphore("sin_done")
    s_mix_high = nc.alloc_semaphore("mix_high")
    s_mix_low = nc.alloc_semaphore("mix_low")
    s_hid_val = nc.alloc_semaphore("hid_val")
    s_hid_high = nc.alloc_semaphore("hid_high")
    s_hid_low = nc.alloc_semaphore("hid_low")
    s_x_back = nc.alloc_semaphore("x_back")
    s_stored = nc.alloc_semaphore("stored")
    s_y_scale = nc.alloc_semaphore("y_scale")
    s_setup = nc.alloc_semaphore("setup")
    loaded = [nc.alloc_semaphore(f"loaded{i}") for i in range(RING)]
    bank_full = [nc.alloc_semaphore(f"bank_full{i}") for i in range(8)]
    bank_free = [nc.alloc_semaphore(f"bank_free{i}") for i in range(8)]

    def full(key):
        return bank_full[USE[key][0]], USE[key][2]

    def drained(key):
        return bank_free[USE[key][0]], USE[key][1] + 1

    def earlier(key):
        return bank_free[USE[key][0]], USE[key][1]

    def tile_full(g, j):
        if j < 3:
            return full(("dense", g, j))
        return s_block_used, GROUPS[g]["first"] + GROUPS[g]["n"]

    def bank_of(key):
        return bank[USE[key][0]]

    def freed(key):
        return bank_free[USE[key][0]]

    def filled(key):
        return bank_full[USE[key][0]]

    def group(tag, **m):
        return next(g for g in GROUPS if g["tag"] == tag and all(g.get(k) == v for k, v in m.items()))

    def group_drained(g):
        return [drained(("dense", g["index"], j)) for j in range(4)]

    def group_turned(g):
        return [drained(("rope", g["index"], j)) for j in range(4)]

    def geometry(kind, a, i):
        first = max(i - 1, 0) if kind == "dil" and a == 0 else 0
        return first, i + 1 - first

    def mask_of(kind, a, i, kb):
        if kind == "dil":
            if a == 0:
                return "causal" if kb == i else "prev"
            return ("mod4", "mod16")[a - 1] + ("d" if kb == i else "")
        return {"diff": "chunk", "sb": "strict", "fox": "causal"}[kind] if kb == i else None

    def p_slot(kind, n, a):
        return (n % 2) * (3 if kind == "dil" else 2) + a

    def operand(g):
        if g["tag"] == "o" or (g["tag"] == "mix" and g["which"] == 1):
            return y_hl
        if g["tag"] == "mix":
            return lru_hl
        return hid_hl if g["tag"] == "down" else act_hl

    def qkv(l, kind):
        if kind == "dil":
            return q2, k2, v2
        slot = (len(KINDS) * l + KINDS.index(kind)) % 2
        return qT[:, slot], kT[:, slot], vv

    LAST = [group("o", l=l, ki=len(KINDS) - 1, m=1)["index"] for l in range(DEPTH)]
    LAST += [group("o2", m=1)["index"], group("down", m=1)["index"]]

    AFTER_NORM = {("q", 0, 0, 0): 0, ("q", 1, 0, 0): 1, ("xr", 0, 0, 0): 2, ("ffn", 0, 0, 0): 3}

    def values_before(gi):
        n = 0
        for st in STEPS:
            if st == ("drain", gi):
                return n
            if st[0] == "att" and 0 <= st[3] - 2 < 16 and st[4] == 0:
                n += len(value_maps(st[2]))

    def values_of_slot(l, ki):
        last = len(KINDS) * l + ki - 1
        return USE["map", last // len(KINDS), KINDS[last % len(KINDS)], 0, 0] if last > 0 else 0

    def prev_kind(l, kind):
        order = [(i, k) for i in range(DEPTH) for k in KINDS]
        return order[order.index((l, kind)) - 1]

    def norm_blocks(i):
        n = 0
        for st in STEPS:
            if st[:2] == ("norm", i):
                return n
            n += st[0] == "block" and st[4][-1] == 3

    def o_end(l, kind):
        order = [(i, k) for i in range(DEPTH) for k in KINDS] + [(2, "dil")]
        pl, pk = order[order.index((l, kind)) - 1]
        g = group("o", l=pl, kind=pk, m=1)
        return g["first"] + g["n"]

    def ready(pe, l, kind):
        if kind == "dil":
            for g in range(G2):
                for done_tile in group_turned(group("q2", g=g)):
                    pe.wait_ge(*done_tile)
                for done_tile in group_turned(group("k2", g=g)):
                    pe.wait_ge(*done_tile)
            return
        for tag in ("q", "k"):
            for done_tile in (group_turned if kind == "diff" else group_drained)(group(tag, l=l, kind=kind)):
                pe.wait_ge(*done_tile)
        if kind == "fox":
            pe.wait_ge(s_ck_ready, l + 1)

    def values_ready(pe, l, kind):
        for v in ([group("v2", g=g) for g in range(G2)] if kind == "dil" else [group("v", l=l, kind=kind)]):
            for done_tile in group_drained(v):
                pe.wait_ge(*done_tile)

    FIRST = [(ident, ident_in), (g_pre, gains)]
    CONSTS = [(mask_b, masks), (sel, sel_in), (wff, w_ff),
              (fb, f_bias), (lv, lam_vec), (sub_g, subln), (rope_1, rope1), (posi, positions),
              (invf, inv_freq), (cw, conv_w), (cb, conv_b), (bg, b_gates), (lam8[:, 0], lru_lambda)]

    def whole(t):
        return t if isinstance(t, bass.AP) else t[tuple(slice(None) for _ in t.shape)]

    with nc.Block() as block:

        @block.sync
        def _(sp):
            for t in range(TT):
                sp.dma_start(x_res[:, t, :], x.rearrange("b (t p) d -> p (b t) d", p=P)[:, t, :]).then_inc(x_in[t], 16)
                if t == 0:
                    for dst, src in FIRST:
                        sp.dma_start(whole(dst), whole(src)).then_inc(s_first, 16)
            for b in range(RING):
                if b == 2:
                    for dst, src in CONSTS:
                        sp.dma_start(whole(dst), whole(src)).then_inc(s_consts, 16)
                sp.dma_start(w_raw[:, b, :], wstream[b]).then_inc(loaded[b], 16)
            with sp.Fori(1, NB // RING) as turn:
                for slot in range(RING):
                    sp.wait_ge(s_block_used, turn * RING + slot - RING + 1)
                    sp.dma_start(w_raw[:, slot, :], wstream[bass.ds(turn * RING + slot, 1)].rearrange("a p n -> (a p) n"))\
                        .then_inc(loaded[slot], 16)
            for b in range(NB // RING * RING, NB):
                sp.wait_ge(s_block_used, b - RING + 1)
                sp.dma_start(w_raw[:, b % RING, :], wstream[b]).then_inc(loaded[b % RING], 16)
            for t in range(TT):
                sp.wait_ge(s_x_new, 3 * TT + t + 1)
                sp.dma_start(out.rearrange("b (t p) d -> p (b t) d", p=P)[:, t, :], x_res[:, t, :]).then_inc(s_stored, 16)
            sp.wait_ge(s_stored, 16 * TT)

        @block.gpsimd
        def _(pool):
            def low(b, slot):
                pool.wait_ge(s_high_done, b + 1)
                nc.gpsimd.tensor_tensor(
                    w_hl[:, slot, 1].rearrange("p c n -> p (c n)"), w_raw[:, slot, :],
                    w_hl[:, slot, 0].rearrange("p c n -> p (c n)").bitcast(f32),
                    ALU.subtract).then_inc(s_low_done, 1)

            with pool.Fori(0, NB // RING) as turn:
                for slot in range(RING):
                    low(turn * RING + slot, slot)
            for b in range(NB // RING * RING, NB):
                low(b, b % RING)

        @block.tensor
        def _(pe):
            def three(out_ap, hi, lo, feat, start, stop):
                (wh, wl), (ah, al) = hi, lo
                if feat:
                    pe.matmul(out_ap, wh, ah, start=start, stop=False)
                    pe.matmul(out_ap, wh, al, start=False, stop=False)
                    return pe.matmul(out_ap, wl, ah, start=False, stop=stop)
                pe.matmul(out_ap, ah, wh, start=start, stop=False)
                pe.matmul(out_ap, ah, wl, start=False, stop=False)
                return pe.matmul(out_ap, al, wh, start=False, stop=stop)

            def product(b, gi, k, tiles):
                g = GROUPS[gi]
                A, w = operand(g), w_hl[:, b % RING]
                if tiles[0] == 0:
                    last = (k + 1) * BC
                    if g["tag"] == "o":
                        pe.wait_ge(s_y_low, MARKS["y_low", (g["l"], g["kind"], last - 1)])
                    if g["tag"] == "mix":
                        if g["which"] == 0:
                            pe.wait_ge(s_lru_low, last)
                        else:
                            pe.wait_ge(*drained(("Y", 2, "dil", last - 1)))
                    if g["tag"] == "o2":
                        pe.wait_ge(s_mix_low, last)
                    if g["tag"] == "down":
                        pe.wait_ge(s_hid_low, last)
                if tiles[0] == 0 and (g["tag"], g.get("l", 0), g.get("ki", 0), g.get("m", 0)) in AFTER_NORM:
                    for c in range(k * BC, (k + 1) * BC):
                        pe.wait_ge(*drained(("norm", AFTER_NORM[g["tag"], g.get("l", 0), g.get("ki", 0), g.get("m", 0)], c)))
                if tiles[0] == 0:
                    pe.wait_ge(s_low_done, b + 1)
                for j in tiles:
                    if k == 0:
                        if earlier(("dense", gi, j))[1] > 0:
                            pe.wait_ge(*earlier(("dense", gi, j)))
                    js = slice(j * P, (j + 1) * P)
                    for cc in range(BC):
                        c, feat = k * BC + cc, g["orient"] == "feat"
                        ws, as_ = (js, slice(None)) if feat else (slice(None), js)
                        mm = three(bank[j][:, :], (w[:, 0, cc, ws], w[:, 1, cc, ws]),
                                   (A[:, c, 0, as_], A[:, c, 1, as_]), feat,
                                   start=(c == 0), stop=(c == g["n"] * BC - 1))
                    if k == g["n"] - 1 and j < 3:
                        mm.then_inc(filled(("dense", gi, j)), 1)
                if tiles[-1] == 3:
                    mm.then_inc(s_block_used, 1)

            def norm_turn(i, part):
                for c in NORM_CHUNKS[part]:
                    if earlier(("norm", i, c))[1] > 0:
                        pe.wait_ge(*earlier(("norm", i, c)))
                for t in range(TT):
                    if part == 0:
                        pe.wait_ge(s_h_rows, i * TT + t + 1)
                    for c in NORM_CHUNKS[part]:
                        tr = pe.matmul(bank_of(("norm", i, c))[:, t * P:(t + 1) * P], x_res[:, t, c * P:(c + 1) * P],
                                       diag[:, t, :], start=True, stop=True)
                        if t == TT - 1:
                            tr.then_inc(filled(("norm", i, c)), 1)

            def forget(l):
                if earlier(("ff", l))[1] > 0:
                    pe.wait_ge(*earlier(("ff", l)))
                to = bank_of(("ff", l))
                pe.wait_ge(s_ff_split, l + 1)
                for c in range(DC):
                    mm = three(to[0:8, :], (wff_hl[:, 0, c], wff_hl[:, 1, c]), (act_hl[:, c, 0, :], act_hl[:, c, 1, :]),
                               True, start=(c == 0), stop=(c == DC - 1))
                mm.then_inc(filled(("ff", l)), 1)

            def rope_turn(gi, nth):
                pe.wait_ge(s_roped, nth)
                if nth == 1:
                    pe.wait_ge(s_first, 16 * len(FIRST))
                for j in range(4):
                    if earlier(("rope", gi, j))[1] > 0:
                        pe.wait_ge(*earlier(("rope", gi, j)))
                    to = bank_of(("rope", gi, j))
                    for t in range(TT):
                        tr = pe.transpose(to[:, t * P:(t + 1) * P], tok_tmp[:, t, j * P:(j + 1) * P], ident[:, :])
                    tr.then_inc(filled(("rope", gi, j)), 1)

            def scores(l, kind, n):
                q, k, _ = qkv(l, kind)
                p, i = n // 4, n % 4
                for a in unit_maps(kind):
                    first, nb = geometry(kind, a, i)
                    if earlier(("S", l, kind, n, a))[1] > 0:
                        pe.wait_ge(*earlier(("S", l, kind, n, a)))
                    to = bank_of(("S", l, kind, n, a))
                    rows = slice(0, P) if kind == "dil" else slice(a * HD, (a + 1) * HD)
                    ch = a * H2 + p if kind == "dil" else p
                    pe.matmul(to[:, 0:nb * P], q[rows, ch, i * P:(i + 1) * P],
                              k[rows, ch, first * P:(first + nb) * P], start=True, stop=False)
                    if kind == "fox":
                        pe.matmul(to[:, 0:nb * P], sel_r[:, 2 * p + a:2 * p + a + 1].broadcast_to([P, P]), ck[:, 0:nb * P],
                                  start=False, stop=False)
                    masked = [kb for kb in range(first, first + nb) if mask_of(kind, a, i, kb)]
                    for kb in masked:
                        cols = slice((kb - first) * P, (kb - first + 1) * P)
                        mm = pe.matmul(to[:, cols], mask_b[:, len(MASKS), :],
                                       mask_b[:, MASKS.index(mask_of(kind, a, i, kb)), :],
                                       start=False, stop=(kb == masked[-1]))
                    mm.then_inc(filled(("S", l, kind, n, a)), 1)

            def turn(l, kind, n, a):
                _, nb = geometry(kind, a, n % 4)
                if earlier(("T", l, kind, n, a))[1] > 0:
                    pe.wait_ge(*earlier(("T", l, kind, n, a)))
                to = bank_of(("T", l, kind, n, a))
                if kind in ("diff", "sb"):
                    pe.wait_ge(s_soft, MARKS["soft", (l, kind, n, a)])
                else:
                    pe.wait_ge(*drained(("S", l, kind, n, a)))
                for kb in range(nb):
                    tr = pe.transpose(to[:, kb * P:(kb + 1) * P],
                                      probs[:, p_slot(kind, n, a), kb * P:(kb + 1) * P], ident[:, :])
                tr.then_inc(filled(("T", l, kind, n, a)), 1)

            def values(l, kind, n):
                _, _, v = qkv(l, kind)
                p, i = n // 4, n % 4
                if earlier(("O", l, kind, n))[1] > 0:
                    pe.wait_ge(*earlier(("O", l, kind, n)))
                to = bank_of(("O", l, kind, n))
                for a in value_maps(kind):
                    first, nb = geometry(kind, a, i)
                    pe.wait_ge(*drained(("T", l, kind, n, a)))
                    half = slice(a * HD, (a + 1) * HD) if kind in ("sb", "fox") else slice(0, P)
                    at_ = (a * H2 + p) * P if kind == "dil" else p * P + half.start
                    one = kind != "dil" or a == 0
                    end = kind != "dil" or a == 2
                    for kb in range(nb):
                        mm = pe.matmul(to[:, half], probs_t[:, USE["map", l, kind, n, a] % 3, kb * P:(kb + 1) * P],
                                       v[:, first + kb, at_:at_ + half.stop - half.start],
                                       start=(one and kb == 0), stop=(end and kb == nb - 1))
                    mm.then_inc(s_pv_done, 1)

            def heads_turn(l, kind, p):
                if earlier(("Y", l, kind, p))[1] > 0:
                    pe.wait_ge(*earlier(("Y", l, kind, p)))
                to = bank_of(("Y", l, kind, p))
                pe.wait_ge(*drained(("O", l, kind, 4 * p + 3)))
                for i in range(TT):
                    tr = pe.transpose(to[:, i * P:(i + 1) * P], y_tok[:, p % 2, i, :], ident[:, :])
                tr.then_inc(filled(("Y", l, kind, p)), 1)

            def gates(c):
                if c == 0:
                    pe.wait_ge(s_wg_in, 16)
                pe.wait_ge(s_conv_done, c + 1)
                for w, name in enumerate("ri"):
                    if earlier((name, c))[1] > 0:
                        pe.wait_ge(*earlier((name, c)))
                    to = bank_of((name, c))
                    pe.matmul(to[:, :], wg[:, w * DC + c, :], xc[:, c, :], start=True, stop=True)\
                        .then_inc(filled((name, c)), 1)

            ropes = 0
            for st in STEPS:
                if st[0] == "block":
                    product(*st[1:])
                elif st[0] == "normturn":
                    norm_turn(*st[1:])
                elif st[0] == "forget":
                    forget(st[1])
                elif st[0] == "ropeturn":
                    ropes += 1
                    rope_turn(st[1], ropes)
                    if ropes == 1:
                        pe.wait_ge(s_consts, 16 * len(CONSTS))
                elif st[:2] == ("lru", "decide"):
                    gates(st[2])
                elif st[0] == "att":
                    _, l, kind, n, part = st
                    if part == 0:
                        if n == 0:
                            ready(pe, l, kind)
                        if n == 2:
                            values_ready(pe, l, kind)
                        if n < 16:
                            scores(l, kind, n)
                        if 0 <= n - 1 < 16:
                            turn(l, kind, n - 1, 0)
                        if 0 <= n - 2 < 16:
                            values(l, kind, n - 2)
                    else:
                        if 0 <= n - 1 < 16:
                            for a in value_maps(kind)[1:]:
                                turn(l, kind, n - 1, a)
                        if n in HEADS_AT:
                            heads_turn(l, kind, HEADS_AT.index(n))

        @block.scalar
        def _(act):
            step = [0]

            def link(ins):
                step[0] += 1
                ins.then_inc(s_act_step, 1)
                act.wait_ge(s_act_step, step[0])

            def high(b):
                if b >= NB:
                    return
                act.wait_ge(loaded[b % RING], 16 * (b // RING + 1))
                nc.scalar.activation(w_hl[:, b % RING, 0].rearrange("p c n -> p (c n)"), w_raw[:, b % RING, :],
                                     ACT.Copy).then_inc(s_high_done, 1)

            def row_scale(src, t, at_, first=None):
                lo = 0 if first is None else D // 2
                link(nc.scalar.activation(probs[:, 0:2, :].rearrange("p a s -> p (a s)")[:, lo:D], src[:, t, lo:D],
                                          ACT.Square, accum_out=stat[:, at_ + t:at_ + t + 1]))
                link(nc.scalar.activation(stat[:, at_ + 4 + t:at_ + 5 + t], stat[:, at_ + t:at_ + t + 1], ACT.Ln,
                                          bias=eps[:, 0:1] if first is None else first, scale=1.0 / D))
                return nc.scalar.activation(stat[:, at_ + 8 + t:at_ + 9 + t], stat[:, at_ + 4 + t:at_ + 5 + t],
                                            ACT.Exp, scale=-0.5)

            def norm_row(i, t):
                if i == 0:
                    act.wait_ge(x_in[t], 16)
                else:
                    act.wait_ge(s_x_new, (i - 1) * TT + t + 1)
                row_scale(x_res, t, 0).then_inc(s_h_scale, 1)

            def norm(i):
                if i == 0:
                    act.preload_act_table_set("natural_log_exp_and_others")
                    act.wait_ge(s_setup, 1)
                    for t in range(TT):
                        norm_row(0, t)
                    act.wait_ge(s_first, 16 * len(FIRST))
                act.dma_start(g_post[:, :], post_gains[i:i + 1, :].partition_broadcast(P)).then_inc(s_gain_in, 16)
                if i > 0:
                    act.wait_ge(s_block_used, norm_blocks(i))

            def norm_high(i, part):
                for c in NORM_CHUNKS[part]:
                    act.wait_ge(*full(("norm", i, c)))
                    nc.scalar.activation(act_hl[:, c, 0, :], bank_of(("norm", i, c))[:, :], ACT.Copy,
                                         scale=g_pre[:, i, c:c + 1]).then_inc(s_norm_high, 1)

            def forget(l):
                act.wait_ge(*drained(("ff", l)))
                link(nc.scalar.activation(ff_log, ff_in, ACT.Abs))
                link(nc.scalar.activation(ff_log, ff_log, ACT.Exp, scale=-1.0))
                nc.scalar.activation(ff_log, ff_log, ACT.Ln, bias=ones[0:8, 0:1]).then_inc(s_ff_log, 1)
                act.wait_ge(s_lam_dots, l + 1)
                nc.scalar.activation(lam[:, 2:4], lam[:, 0:2], ACT.Exp).then_inc(s_lam_exp, 1)

            def drain(gi):
                g = GROUPS[gi]
                tag = g["tag"]
                if tag in ("o", "mix", "o2", "down"):
                    return
                if tag == "v":
                    act.wait_ge(s_pv_done, values_before(gi))
                if tag in ("q", "k") and values_of_slot(g["l"], g["ki"]) > 0:
                    act.wait_ge(s_pv_done, values_of_slot(g["l"], g["ki"]))
                if tag in ("q", "k", "q2", "k2") and g["orient"] == "tok":
                    before = [x["index"] for x in GROUPS[:gi] if x["orient"] == "tok" and x["tag"] in ("q", "k", "q2", "k2")]
                    if before:
                        act.wait_ge(*full(("rope", before[-1], 3)))
                if tag == "g" and gi > 4:
                    act.wait_ge(s_y_low, MARKS["y_low", prev_kind(g["l"], g["kind"]) + (3,)])
                slot = (len(KINDS) * g.get("l", 0) + g.get("ki", 0)) % 2
                for j in range(4):
                    act.wait_ge(*tile_full(gi, j))
                    ps = bank[j]
                    done = freed(("dense", gi, j))
                    if tag in ("q", "k", "q2", "k2") and g["orient"] == "tok":
                        nc.scalar.activation(tok_tmp[:, j, :], ps[:, :], ACT.Copy).then_inc(done, 1)
                    elif tag == "q":
                        nc.scalar.activation(qT[:, slot, j, :], ps[:, :], ACT.Copy, scale=HD ** -0.5).then_inc(done, 1)
                    elif tag == "k":
                        nc.scalar.activation(kT[:, slot, j, :], ps[:, :], ACT.Copy).then_inc(done, 1)
                    elif tag == "v":
                        nc.scalar.activation(vv[:, j, :], ps[:, :], ACT.Copy).then_inc(done, 1)
                    elif tag == "v2":
                        nc.scalar.activation(v2[:, j, g["g"] * COLS:(g["g"] + 1) * COLS], ps[:, :], ACT.Copy).then_inc(done, 1)
                    elif tag == "g":
                        nc.scalar.activation(gate[:, j, :], ps[:, :], ACT.Silu).then_inc(done, 1)
                    elif tag == "xr":
                        nc.scalar.activation(xpad[:, 4 * g["m"] + j, PAD:], ps[:, :], ACT.Copy).then_inc(done, 1)
                    elif tag == "gr":
                        nc.scalar.activation(gelu[:, 4 * g["m"] + j, :], ps[:, :], ACT.Gelu_apprx_tanh).then_inc(done, 1)
                    elif tag == "gate" and g["which"] == 0:
                        if j == 0:
                            act.wait_ge(s_spilled, 16)
                        nc.scalar.activation(mix[:, 4 * g["m"] + j, :], ps[:, :], ACT.Sigmoid).then_inc(done, 1)
                    elif tag == "gate":
                        if j == 0:
                            act.wait_ge(s_pv_done, values_before(gi))
                        nc.scalar.activation(sig[:, 4 * g["m"] + j, :], ps[:, :], ACT.Sigmoid).then_inc(done, 1)
                    elif tag == "ffn" and j < 2:
                        n = 2 * g["m"] + j
                        if n - 1 > 0:
                            act.wait_ge(s_hid_val, n - 1)
                        nc.scalar.activation(probs[:, j, :], ps[:, :], ACT.Silu).then_inc(done, 1)
                    elif tag == "ffn":
                        n = 2 * g["m"] + j - 2
                        act.wait_ge(s_hid_val, n + 1)
                        nc.scalar.activation(hid_hl[:, n, 0, :], probs[:, j, :], ACT.Copy).then_inc(s_hid_high, 1)
                if tag == "g":
                    act.preload_act_table_set("natural_log_exp_and_others")

            def rope(gi):
                g = GROUPS[gi]
                for j in range(4):
                    act.wait_ge(*full(("rope", gi, j)))
                    ps = bank_of(("rope", gi, j))
                    scale = {"q": HD ** -0.5, "q2": (2 * HD) ** -0.5}.get(g["tag"], 1.0)
                    slot = (len(KINDS) * g.get("l", 0) + g.get("ki", 0)) % 2
                    dst = {"q": qT[:, slot], "k": kT[:, slot], "q2": q2, "k2": k2}[g["tag"]]
                    nc.scalar.activation(dst[:, g.get("g", 0) * H2 + j, :], ps[:, :], ACT.Copy, scale=scale)\
                        .then_inc(freed(("rope", gi, j)), 1)

            def soften(l, kind, n):
                par = n % 2
                if n >= 2:
                    act.wait_ge(*full(("T", l, kind, n - 2, value_maps(kind)[-1])))
                for a in unit_maps(kind):
                    _, nb = geometry(kind, a, n % 4)
                    row = probs[:, p_slot(kind, n, a), 0:nb * P]
                    if kind == "sb":
                        act.wait_ge(*full(("S", l, kind, n, a)))
                        ps = bank_of(("S", l, kind, n, a))
                        link(nc.scalar.activation(row, ps[:, 0:nb * P], ACT.Abs))
                        link(nc.scalar.activation(row, row, ACT.Exp, scale=-1.0))
                        nc.scalar.activation(row, row, ACT.Ln, bias=ones[:, 0:1]).then_inc(s_abs_log, 1)
                    else:
                        if kind != "dil" or a == 0:
                            act.wait_ge(s_rows_max, MARKS["rows_max", (l, kind, n, a)])
                        b = 0 if kind == "dil" else a
                        nc.scalar.activation(row, bank[USE["S", l, kind, n, a][0]][:, 0:nb * P], ACT.Exp,
                                             bias=nmax[:, par, b:b + 1], accum_out=sums[:, par, a:a + 1])\
                            .then_inc(freed(("S", l, kind, n, a)), 1)

            def break_stick(l, kind, n):
                for a in range(2):
                    _, nb = geometry(kind, a, n % 4)
                    row = probs[:, p_slot(kind, n, a), 0:nb * P]
                    act.wait_ge(*drained(("S", l, kind, n, a)))
                    nc.scalar.activation(row, row, ACT.Exp).then_inc(s_soft, 1)

            def turned(l, kind, n, a):
                _, nb = geometry(kind, a, n % 4)
                m = USE["map", l, kind, n, a]
                act.wait_ge(*full(("T", l, kind, n, a)))
                if m > 2:
                    act.wait_ge(s_pv_done, m - 2)
                nc.scalar.activation(probs_t[:, m % 3, 0:nb * P], bank_of(("T", l, kind, n, a))[:, 0:nb * P], ACT.Copy)\
                    .then_inc(freed(("T", l, kind, n, a)), 1)

            def row_rms(l, n):
                act.wait_ge(s_pv_done, USE["map", l, "diff", n, 0] + 1)
                link(nc.scalar.activation(y_sq[:, :], bank[BO][:, 0:P], ACT.Square, accum_out=stat[:, 16:17]))
                link(nc.scalar.activation(stat[:, 17:18], stat[:, 16:17], ACT.Ln, bias=eps[:, 0:1], scale=1.0 / P))
                nc.scalar.activation(stat[:, 18 + n % 2:19 + n % 2], stat[:, 17:18], ACT.Exp, scale=-0.5)\
                    .then_inc(s_rms, 1)

            def heads(l, kind, p):
                if kind == "dil":
                    act.wait_ge(*full(("Y", l, kind, p)))
                    ps = bank_of(("Y", l, kind, p))
                    src = ps[:, :]
                else:
                    act.wait_ge(*drained(("Y", l, kind, p)))
                    src = y_tmp[:, :]
                if p == 0 and (l, kind) != (0, KINDS[0]):
                    act.wait_ge(s_block_used, o_end(l, kind))
                nc.scalar.activation(y_hl[:, p, 0, :], src, ACT.Copy).then_inc(s_y_high, 1)

            def lru(part, c):
                if part == "decide":
                    if c == 0:
                        link(nc.scalar.activation(lam8[:, 1], lam8[:, 0], ACT.Abs))
                        link(nc.scalar.activation(lam8[:, 1], lam8[:, 1], ACT.Exp, scale=-1.0))
                        nc.scalar.activation(lam8[:, 1], lam8[:, 1], ACT.Ln, bias=ones[:, 0:1]).then_inc(s_lam_log, 1)
                    act.wait_ge(*full(("r", c)))
                    nc.scalar.activation(xpad[:, c, PAD:], bank_of(("r", c))[:, :], ACT.Sigmoid,
                                         bias=bg[:, 0, c:c + 1]).then_inc(freed(("r", c)), 1)
                    act.wait_ge(*full(("i", c)))
                    if c > 1:
                        act.wait_ge(s_ix_done, c - 1)
                    nc.scalar.activation(probs[:, 4 + c % 2, :], bank_of(("i", c))[:, :], ACT.Sigmoid,
                                         bias=bg[:, 1, c:c + 1]).then_inc(freed(("i", c)), 1)
                elif part == "decay":
                    act.wait_ge(*drained(("r", c)))
                    if c == 0:
                        act.wait_ge(s_lam8_ready, 1)
                    nc.scalar.activation(lru_am[:, c, 1, :], xpad[:, c, PAD:], ACT.Tanh, scale=lam8[:, 2, c:c + 1])
                    nc.scalar.activation(lru_am[:, c, 0, :], xpad[:, c, PAD:], ACT.Exp, scale=lam8[:, 2, c:c + 1])\
                        .then_inc(s_exp_done, 1)
                elif part == "scale":
                    act.wait_ge(s_am_done, c + 1)
                    nc.scalar.activation(lru_am[:, c, 1, :], lru_am[:, c, 1, :], ACT.Sqrt, scale=-1.0)\
                        .then_inc(s_mult_done, 1)
                else:
                    act.wait_ge(s_lru_val, c + 1)
                    nc.scalar.activation(lru_hl[:, c, 0, :], gelu[:, c, :], ACT.Copy).then_inc(s_lru_high, 1)

            def first_half(i):
                y = y_ffn if i == 3 else y_acc
                if i == 2:
                    act.wait_ge(s_mix_low, DC)
                    act.dma_start(x_res[:, :, :], x_spill).then_inc(s_x_back, 16)
                for t in range(TT):
                    act.wait_ge(*drained(("dense", LAST[i] - 1, t)))
                    link(nc.scalar.activation(probs[:, 0, :], y[:, t, 0:D // 2], ACT.Square,
                                              accum_out=stat[:, 40 + t:41 + t]))
                link(nc.scalar.activation(stat[:, 44:48], stat[:, 40:44], ACT.Identity, bias=eps[:, 0:1], scale=1.0 / D))

            def post(i):
                y = y_ffn if i == 3 else y_acc
                if i >= 2:
                    act.preload_act_table_set("natural_log_exp_and_others")
                for t in range(TT):
                    act.wait_ge(*drained(("dense", LAST[i], t)))
                    row_scale(y, t, 20, stat[:, 44 + t:45 + t]).then_inc(s_y_scale, 1)
                    if i < 3 and t > 0:
                        norm_row(i + 1, t - 1)
                if i < 3:
                    norm_row(i + 1, TT - 1)

            for st in STEPS:
                if st[0] == "block":
                    if st[4][0] == 0:
                        high(st[1] + 2)
                elif st[0] == "drain":
                    drain(st[1])
                    if st[1] + 1 in LAST:
                        first_half(LAST.index(st[1] + 1))
                elif st[0] == "norm":
                    norm(st[1])
                elif st[0] == "normturn":
                    if st[1:] == (0, 0):
                        high(0)
                    norm_high(*st[1:])
                    if st[1:] == (0, 0):
                        high(1)
                elif st[0] == "forget":
                    forget(st[1])
                elif st[0] == "ropeturn":
                    rope(st[1])
                elif st[0] == "att":
                    _, l, kind, n, part = st
                    if part == 0:
                        if kind == "dil" and n == 0:
                            act.preload_act_table_set("natural_log_exp_and_others")
                        if 0 <= n - 1 < 16:
                            turned(l, kind, n - 1, 0)
                        if n < 16:
                            soften(l, kind, n)
                        if kind == "dil" and 0 <= n - 1 < 16:
                            turned(l, kind, n - 1, 2)
                        if kind == "diff" and 0 <= n - 2 < 16:
                            row_rms(l, n - 2)
                    else:
                        if kind == "sb" and n < 16:
                            break_stick(l, kind, n)
                        if n in HEADS_AT:
                            heads(l, kind, HEADS_AT.index(n))
                elif st[0] == "spill":
                    act.dma_start(x_spill, x_res[:, :, :]).then_inc(s_spilled, 16)
                    act.dma_start(wg, w_gates).then_inc(s_wg_in, 16)
                elif st[0] == "lru":
                    lru(*st[1:])
                elif st[0] == "angles":
                    act.wait_ge(s_ang_ready, 1)
                    nc.scalar.activation(rope_2[:, :, :, :], red[:, :, :, :], ACT.Sin).then_inc(s_sin_done, 1)
                elif st[0] == "mixsplit":
                    for c in range(4 * st[1], 4 * st[1] + 4):
                        act.wait_ge(*drained(("dense", group("mix", m=st[1], which=1)["index"], c % 4)))
                        nc.scalar.activation(act_hl[:, c, 0, :], mix[:, c, :], ACT.Copy).then_inc(s_mix_high, 1)
                elif st[0] == "post":
                    post(st[1])

        @block.vector
        def _(dve):
            step = [0]

            def link(ins):
                step[0] += 1
                ins.then_inc(s_dve_step, 1)
                dve.wait_ge(s_dve_step, step[0])

            def setup():
                link(nc.vector.memset(ones[:, :], 1.0))
                link(nc.vector.memset(ck[:, :].bitcast(f32), 0.0))
                link(nc.vector.memset(eps[:, :], EPS))
                nc.vector.memset(sums[:, :, :], 0.0).then_inc(s_setup, 1)
                dve.wait_ge(s_setup, 1)

            def setup_constants():
                dve.wait_ge(s_consts, 16 * len(CONSTS))
                link(nc.vector.tensor_copy(sel_r[:, :], sel[:, :]))
                for l in range(DEPTH):
                    link(nc.vector.tensor_scalar(sub_g[:, l:l + 1], sub_g[:, l:l + 1], 1.0 - LAM_INIT[l], None, ALU.mult))

            def norm_row(i, t):
                dve.wait_ge(s_h_scale, i * TT + t + 1)
                nc.vector.tensor_scalar(diag[:, t, :], ident[:, :], stat[:, 8 + t:9 + t], None, ALU.mult)\
                    .then_inc(s_h_rows, 1)

            def norm(i):
                if i == 0:
                    dve.wait_ge(s_first, 16 * len(FIRST))
                    for t in range(TT):
                        norm_row(0, t)

            def norm_low(i, part):
                for c in NORM_CHUNKS[part]:
                    dve.wait_ge(s_norm_high, i * DC + c + 1)
                    nc.vector.scalar_tensor_tensor(
                        out=act_hl[:, c, 1, :], in0=bank[4 + c % 4][:, :], scalar=g_pre[:, i, c:c + 1],
                        in1=act_hl[:, c, 0, :].bitcast(f32), op0=ALU.mult, op1=ALU.subtract)\
                        .then_inc(freed(("norm", i, c)), 1)

            def forget_weights(l):
                link(nc.vector.tensor_copy(wff_hl[:, 0], wff[:, l]))
                nc.vector.tensor_tensor(wff_hl[:, 1], wff[:, l], wff_hl[:, 0].bitcast(f32), ALU.subtract)\
                    .then_inc(s_ff_split, 1)
                prod = y_tmp[:, 0:2 * HD].rearrange("p (a d) -> p a d", a=2)
                link(nc.vector.tensor_tensor(prod, lv[:, l, 0::2, :], lv[:, l, 1::2, :], ALU.mult))
                nc.vector.tensor_reduce(lam[:, 0:2], prod, AX.X, ALU.add).then_inc(s_lam_dots, 1)

            def forget(l):
                dve.wait_ge(*full(("ff", l)))
                ps = bank_of(("ff", l))
                nc.vector.tensor_scalar(ff_in, ps[0:8, :], fb[0:8, l:l + 1], None, ALU.add).then_inc(freed(("ff", l)), 1)
                dve.wait_ge(s_lam_exp, l + 1)
                link(nc.vector.tensor_tensor(lam[:, 5:6], lam[:, 3:4], lam[:, 2:3], ALU.subtract))
                link(nc.vector.tensor_scalar(lam[:, 4:5], lam[:, 5:6], -LAM_INIT[l], None, ALU.add))
                dve.wait_ge(s_ff_log, l + 1)
                dve.wait_ge(*drained(("ff", l)))
                link(nc.vector.scalar_tensor_tensor(out=ff_in, in0=ff_in, scalar=0.0, in1=ff_log,
                                                    op0=ALU.min, op1=ALU.subtract))
                link(nc.vector.tensor_tensor_scan(ckf[0:8, :], ones[0:8, 0:1].broadcast_to([8, S]), ff_in,
                                                  0.0, ALU.mult, ALU.subtract))
                link(nc.vector.tensor_copy(ck[0:8, :], ckf[0:8, :]))
                nc.vector.tensor_tensor(ck[32:40, :], ckf[0:8, :], ck[0:8, :].bitcast(f32), ALU.subtract)\
                    .then_inc(s_ck_ready, 1)
                dve.wait_ge(s_ck_ready, l + 1)

            def drain(gi, tiles=range(4)):
                g = GROUPS[gi]
                tag = g["tag"]
                if tag not in ("o", "mix", "ffn", "o2", "down"):
                    return
                for j in tiles:
                    if tag == "ffn" and j < 2:
                        continue
                    dve.wait_ge(*tile_full(gi, j))
                    ps = bank[j]
                    done = freed(("dense", gi, j))
                    if tag == "o":
                        dst = y_acc[:, j, g["m"] * COLS:(g["m"] + 1) * COLS]
                        if g["ki"] == 0:
                            nc.vector.tensor_copy(dst, ps[:, :]).then_inc(done, 1)
                        else:
                            dve.wait_ge(*drained(("dense", group("o", l=g["l"], ki=g["ki"] - 1, m=g["m"])["index"], j)))
                            nc.vector.tensor_tensor(dst, ps[:, :], dst, ALU.add).then_inc(done, 1)
                    elif tag == "o2":
                        nc.vector.tensor_copy(y_acc[:, j, g["m"] * COLS:(g["m"] + 1) * COLS], ps[:, :]).then_inc(done, 1)
                    elif tag == "down":
                        nc.vector.tensor_copy(y_ffn[:, j, g["m"] * COLS:(g["m"] + 1) * COLS], ps[:, :]).then_inc(done, 1)
                    elif tag == "mix":
                        gates = group("gate", m=g["m"], which=g["which"])["index"]
                        dve.wait_ge(*drained(("dense", gates, j)))
                        dst = mix[:, 4 * g["m"] + j, :]
                        if g["which"] == 0:
                            nc.vector.tensor_tensor(dst, ps[:, :], dst, ALU.mult).then_inc(done, 1)
                        else:
                            link(nc.vector.tensor_tensor(y_tmp[:, :], ps[:, :], sig[:, 4 * g["m"] + j, :], ALU.mult))
                            nc.vector.tensor_tensor(dst, dst, y_tmp[:, :], ALU.add).then_inc(done, 1)
                            dve.wait_ge(*drained(("dense", gi, j)))
                    elif tag == "ffn":
                        n = 2 * g["m"] + j - 2
                        dve.wait_ge(*drained(("dense", gi, j - 2)))
                        if n - 1 > 0:
                            dve.wait_ge(s_hid_low, n - 1)
                        link(nc.vector.tensor_tensor(probs[:, j, :], ps[:, :], probs[:, j - 2, :], ALU.mult))
                        dve.sem_inc(s_hid_val, 1)
                        dve.sem_inc(done, 1)
                        dve.wait_ge(s_hid_high, n + 1)
                        nc.vector.tensor_tensor(hid_hl[:, n, 1, :], probs[:, j, :], hid_hl[:, n, 0, :].bitcast(f32),
                                                ALU.subtract).then_inc(s_hid_low, 1)

            def rope(gi, nth):
                g = GROUPS[gi]
                for t in range(TT):
                    dve.wait_ge(*drained(("dense", gi, t)))
                if g["tag"] in ("q2", "k2"):
                    dve.wait_ge(s_sin_done, 1)
                F, table = (2 * HD, rope_2) if g["tag"] in ("q2", "k2") else (HD, rope_1)
                nh, half = COLS // F, table.shape[3]
                rows = tok_tmp.rearrange("p t (h f) -> p t h f", f=F)
                r1, r2 = rows[:, :, :, 0:half], rows[:, :, :, half:2 * half]
                c = table[:, 0].unsqueeze(2).broadcast_to([P, TT, nh, half])
                s = table[:, 1].unsqueeze(2).broadcast_to([P, TT, nh, half])
                tmp = y_tok[:, :, :, :].rearrange("p a t f -> p (a t f)").rearrange(
                    "p (k t h f) -> p k t h f", k=4, t=TT, h=nh)
                link(nc.vector.tensor_tensor(tmp[:, 0], r1, c, ALU.mult))
                link(nc.vector.tensor_tensor(tmp[:, 1], r2, s, ALU.mult))
                link(nc.vector.tensor_tensor(tmp[:, 2], r2, c, ALU.mult))
                link(nc.vector.tensor_tensor(tmp[:, 3], r1, s, ALU.mult))
                link(nc.vector.tensor_tensor(r1, tmp[:, 0], tmp[:, 1], ALU.subtract))
                nc.vector.tensor_tensor(r2, tmp[:, 2], tmp[:, 3], ALU.add).then_inc(s_roped, 1)
                dve.wait_ge(s_roped, nth)

            def stick(l, kind, n, a):
                _, nb = geometry(kind, a, n % 4)
                row = probs[:, p_slot(kind, n, a), 0:nb * P]
                back = row[:, ::-1]
                ps = bank_of(("S", l, kind, n, a))
                dve.wait_ge(*full(("S", l, kind, n, a)))
                dve.wait_ge(s_abs_log, MARKS["abs_log", (l, kind, n, a)])
                link(nc.vector.scalar_tensor_tensor(out=row, in0=ps[:, 0:nb * P], scalar=0.0, in1=row,
                                                    op0=ALU.max, op1=ALU.add))
                link(nc.vector.tensor_tensor_scan(back, ones[:, 0:1].broadcast_to([P, nb * P]), back,
                                                  0.0, ALU.mult, ALU.add))
                nc.vector.tensor_tensor(row, ps[:, 0:nb * P], row, ALU.subtract)\
                    .then_inc(freed(("S", l, kind, n, a)), 1)

            def maxima(l, kind, n):
                par = n % 2
                for a in unit_maps(kind):
                    _, nb = geometry(kind, a, n % 4)
                    dve.wait_ge(*full(("S", l, kind, n, a)))
                    ps = bank_of(("S", l, kind, n, a))
                    if kind == "dil":
                        link(nc.vector.tensor_reduce(stat[:, 32 + a:33 + a], ps[:, 0:nb * P], AX.X, ALU.max))
                    else:
                        nc.vector.tensor_reduce(nmax[:, par, a:a + 1], ps[:, 0:nb * P], AX.X, ALU.max, negate=True)\
                            .then_inc(s_rows_max, 1)
                if kind == "dil":
                    nc.vector.tensor_reduce(nmax[:, par, 0:1], stat[:, 32:35], AX.X, ALU.max, negate=True)\
                        .then_inc(s_rows_max, 1)

            def inverses(l, kind, n):
                par = n % 2
                for a in unit_maps(kind):
                    dve.wait_ge(*drained(("S", l, kind, n, a)))
                if kind == "dil":
                    link(nc.vector.tensor_reduce(stat[:, 36:37], sums[:, par, 0:3], AX.X, ALU.add))
                    link(nc.vector.reciprocal(rinv[:, n % 4, 0:1], stat[:, 36:37]))
                    return
                link(nc.vector.reciprocal(rinv[:, n % 4, 0:2], sums[:, par, 0:2]))
                if kind == "diff":
                    _, nb = geometry(kind, 0, n % 4)
                    r0, r1 = (probs[:, p_slot(kind, n, a), 0:nb * P] for a in range(2))
                    link(nc.vector.tensor_tensor(rinv[:, n % 4, 1:2], rinv[:, n % 4, 1:2], lam[:, 4:5], ALU.mult))
                    link(nc.vector.tensor_scalar(r0, r0, rinv[:, n % 4, 0:1], None, ALU.mult))
                    nc.vector.scalar_tensor_tensor(out=r0, in0=r1, scalar=rinv[:, n % 4, 1:2], in1=r0,
                                                   op0=ALU.mult, op1=ALU.add).then_inc(s_soft, 1)

            def turned(l, kind, n):
                _, nb = geometry(kind, 1, n % 4)
                m = USE["map", l, kind, n, 1]
                dve.wait_ge(*full(("T", l, kind, n, 1)))
                if m > 2:
                    dve.wait_ge(s_pv_done, m - 2)
                nc.vector.tensor_copy(probs_t[:, m % 3, 0:nb * P], bank_of(("T", l, kind, n, 1))[:, 0:nb * P])\
                    .then_inc(freed(("T", l, kind, n, 1)), 1)

            def outputs(l, kind, n):
                p, i = n // 4, n % 4
                dve.wait_ge(s_pv_done, USE["map", l, kind, n, value_maps(kind)[-1]] + 1)
                if i == 0 and p >= 2:
                    dve.wait_ge(*full(("Y", l, kind, p - 2)))
                dst = y_tok[:, p % 2, i, :]
                o = bank[BO]
                done = freed(("O", l, kind, n))
                if kind == "diff":
                    dve.wait_ge(s_rms, MARKS["rms", (l, kind, n)])
                    nc.vector.tensor_scalar(dst, o[:, 0:P], stat[:, 18 + n % 2:19 + n % 2], None, ALU.mult).then_inc(done, 1)
                elif kind == "sb":
                    nc.vector.tensor_copy(dst, o[:, 0:P]).then_inc(done, 1)
                elif kind == "dil":
                    nc.vector.tensor_scalar(dst, o[:, 0:P], rinv[:, n % 4, 0:1], None, ALU.mult).then_inc(done, 1)
                else:
                    nc.vector.tensor_scalar(dst[:, 0:HD], o[:, 0:HD], rinv[:, n % 4, 0:1], None, ALU.mult)
                    nc.vector.tensor_scalar(dst[:, HD:P], o[:, HD:P], rinv[:, n % 4, 1:2], None, ALU.mult).then_inc(done, 1)

            def heads(l, kind, p):
                dve.wait_ge(*full(("Y", l, kind, p)))
                ps = bank_of(("Y", l, kind, p))
                if kind == "dil":
                    dve.wait_ge(s_y_high, MARKS["y_high", (l, kind, p)])
                    nc.vector.tensor_tensor(y_hl[:, p, 1, :], ps[:, :], y_hl[:, p, 0, :].bitcast(f32), ALU.subtract)\
                        .then_inc(freed(("Y", l, kind, p)), 1)
                    return
                if p == 0:
                    for done_tile in group_drained(group("g", l=l, kind=kind)):
                        dve.wait_ge(*done_tile)
                scalar = sub_g[:, l:l + 1] if kind == "diff" else 1.0
                nc.vector.scalar_tensor_tensor(out=y_tmp[:, :], in0=ps[:, :], scalar=scalar, in1=gate[:, p, :],
                                               op0=ALU.mult, op1=ALU.mult).then_inc(freed(("Y", l, kind, p)), 1)
                dve.wait_ge(s_y_high, MARKS["y_high", (l, kind, p)])
                dve.wait_ge(*drained(("Y", l, kind, p)))
                nc.vector.tensor_tensor(y_hl[:, p, 1, :], y_tmp[:, :], y_hl[:, p, 0, :].bitcast(f32), ALU.subtract)\
                    .then_inc(s_y_low, 1)
                dve.wait_ge(s_y_low, MARKS["y_low", (l, kind, p)])

            def convolve(c):
                if c % 4 == 0:
                    for done_tile in group_drained(group("xr", m=c // 4)):
                        dve.wait_ge(*done_tile)
                dst = xc[:, c, :]
                link(nc.vector.tensor_scalar(dst, xpad[:, c, 1:1 + S], cw[:, c, 0:1], cb[:, c:c + 1], ALU.mult, ALU.add))
                for j in range(1, 3):
                    link(nc.vector.scalar_tensor_tensor(out=dst, in0=xpad[:, c, 1 + j:1 + j + S], scalar=cw[:, c, j:j + 1],
                                                        in1=dst, op0=ALU.mult, op1=ALU.add))
                nc.vector.scalar_tensor_tensor(out=dst, in0=xpad[:, c, 4:4 + S], scalar=cw[:, c, 3:4], in1=dst,
                                               op0=ALU.mult, op1=ALU.add).then_inc(s_conv_done, 1)

            def lru_low(c):
                dve.wait_ge(s_lru_high, c + 1)
                nc.vector.tensor_tensor(lru_hl[:, c, 1, :], gelu[:, c, :], lru_hl[:, c, 0, :].bitcast(f32), ALU.subtract)\
                    .then_inc(s_lru_low, 1)

            def lru(part, c):
                if part == "decide":
                    if c == 0:
                        dve.wait_ge(s_lam_log, 1)
                        link(nc.vector.tensor_scalar(lam8[:, 2], lam8[:, 0], -1.0, 0.0, ALU.mult, ALU.max))
                        link(nc.vector.tensor_tensor(lam8[:, 2], lam8[:, 2], lam8[:, 1], ALU.add))
                        nc.vector.tensor_scalar(lam8[:, 2], lam8[:, 2], -8.0, None, ALU.mult).then_inc(s_lam8_ready, 1)
                        link(nc.vector.memset(xpad[:, :, 0:PAD], 0.0))
                        convolve(0)
                    if c + 1 < DC:
                        convolve(c + 1)
                    dve.wait_ge(*drained(("i", c)))
                    nc.vector.tensor_tensor(xc[:, c, :], probs[:, 4 + c % 2, :], xc[:, c, :], ALU.mult).then_inc(s_ix_done, 1)
                elif part == "decay":
                    dve.wait_ge(s_exp_done, c + 1)
                    link(nc.vector.tensor_tensor(probs_t[:, 0, :], lru_am[:, c, 0, :], lru_am[:, c, 0, :], ALU.mult))
                    nc.vector.scalar_tensor_tensor(out=lru_am[:, c, 1, :], in0=probs_t[:, 0, :], scalar=1.0,
                                                   in1=lru_am[:, c, 1, :], op0=ALU.add, op1=ALU.mult).then_inc(s_am_done, 1)
                    dve.wait_ge(s_am_done, c + 1)
                elif part == "scan":
                    if c % 4 == 0:
                        for done_tile in group_drained(group("gr", m=c // 4)):
                            dve.wait_ge(*done_tile)
                    dve.wait_ge(s_mult_done, c + 1)
                    if c == 0:
                        dve.wait_ge(s_ix_done, DC)
                    link(nc.vector.memset(lru_am[:, c, 1, 0:1], 1.0))
                    link(nc.vector.tensor_tensor(xc[:, c, :], lru_am[:, c, 1, :], xc[:, c, :], ALU.mult))
                    link(nc.vector.tensor_tensor_scan(xpad[:, c, PAD:], lru_am[:, c, 0, :], xc[:, c, :], 0.0, ALU.mult, ALU.add))
                    nc.vector.tensor_tensor(gelu[:, c, :], xpad[:, c, PAD:], gelu[:, c, :], ALU.mult).then_inc(s_lru_val, 1)
                    if c > 0:
                        lru_low(c - 1)
                    if c == DC - 1:
                        dve.wait_ge(s_lru_val, DC)
                        lru_low(c)

            def angles():
                link(nc.vector.tensor_copy(posf[:, :], posi[:, :]))
                hf = ROT2 // 2
                link(nc.vector.tensor_tensor(ang[:, :, :], posf[:, :].unsqueeze(2).broadcast_to([P, TT, hf]),
                                             invf[:, :].unsqueeze(1).broadcast_to([P, TT, hf]), ALU.mult))
                big = 1.5 * 2.0 ** 23
                hi, mid = 6.28125, 0.00193500518798828125
                low = 2 * math.pi - hi - mid
                for s, (off, add) in enumerate(((0.25, math.pi / 2), (0.0, 0.0))):
                    link(nc.vector.tensor_scalar(turns[:, s], ang[:, :, :], 1 / (2 * math.pi), off, ALU.mult, ALU.add))
                    link(nc.vector.tensor_scalar(turns[:, s], turns[:, s], big, None, ALU.add))
                    link(nc.vector.tensor_scalar(turns[:, s], turns[:, s], -big, None, ALU.add))
                    link(nc.vector.scalar_tensor_tensor(out=red[:, s], in0=turns[:, s], scalar=-hi, in1=ang[:, :, :],
                                                        op0=ALU.mult, op1=ALU.add))
                    for part in (mid, low):
                        link(nc.vector.scalar_tensor_tensor(out=red[:, s], in0=turns[:, s], scalar=-part, in1=red[:, s],
                                                            op0=ALU.mult, op1=ALU.add))
                    link(nc.vector.tensor_scalar(red[:, s], red[:, s], add, None, ALU.add))
                PI = 3.1415925
                nc.vector.tensor_scalar(red[:, :, :, :], red[:, :, :, :], PI, -PI, ALU.min, ALU.max).then_inc(s_ang_ready, 1)

            def post(i):
                y = y_ffn if i == 3 else y_acc
                dve.wait_ge(s_gain_in, 16 * (i + 1))
                if i == 2:
                    dve.wait_ge(s_x_back, 16)
                drain(LAST[i], range(1))
                for t in range(TT):
                    if t + 1 < TT:
                        drain(LAST[i], range(t + 1, t + 2))
                    dve.wait_ge(s_y_scale, i * TT + t + 1)
                    link(nc.vector.scalar_tensor_tensor(out=y[:, t, :], in0=y[:, t, :], scalar=stat[:, 28 + t:29 + t],
                                                        in1=g_post[:, :], op0=ALU.mult, op1=ALU.mult))
                    nc.vector.tensor_tensor(x_res[:, t, :], x_res[:, t, :], y[:, t, :], ALU.add).then_inc(s_x_new, 1)
                    if i < 3 and t > 0:
                        norm_row(i + 1, t - 1)
                if i < 3:
                    norm_row(i + 1, TT - 1)

            setup()
            ropes = 0
            for st in STEPS:
                if st[0] == "drain":
                    if st[1] not in LAST:
                        drain(st[1])
                elif st[0] == "norm":
                    norm(st[1])
                elif st[0] == "normturn":
                    norm_low(*st[1:])
                    if st[1:] == (0, 1):
                        setup_constants()
                    if st[1] < DEPTH and st[2] == 1:
                        forget_weights(st[1])
                elif st[0] == "forget":
                    forget(st[1])
                elif st[0] == "rope":
                    ropes += 1
                    rope(st[1], ropes)
                elif st[0] == "att":
                    _, l, kind, n, part = st
                    if part == 0:
                        if n < 16 and kind != "sb":
                            maxima(l, kind, n)
                        if 0 <= n - 2 < 16:
                            outputs(l, kind, n - 2)
                        if n < 16 and kind == "sb":
                            for a in range(2):
                                stick(l, kind, n, a)
                        if n < 16 and kind == "diff":
                            inverses(l, kind, n)
                    else:
                        if 0 <= n - 1 < 16 and kind != "diff":
                            turned(l, kind, n - 1)
                        if n < 16 and kind in ("fox", "dil"):
                            inverses(l, kind, n)
                        if n in HEADS_AT:
                            heads(l, kind, HEADS_AT.index(n))
                elif st[0] == "lru":
                    lru(*st[1:])
                elif st[0] == "angles":
                    angles()
                elif st[0] == "mixsplit":
                    for c in range(4 * st[1], 4 * st[1] + 4):
                        dve.wait_ge(s_mix_high, c + 1)
                        nc.vector.tensor_tensor(act_hl[:, c, 1, :], mix[:, c, :], act_hl[:, c, 0, :].bitcast(f32),
                                                ALU.subtract).then_inc(s_mix_low, 1)
                elif st[0] == "post":
                    post(st[1])


def kernel(**inputs):
    import concourse.bacc as bacc
    import ml_dtypes
    from concourse.bass_utils import run_bass_kernel_spmd

    a = {k: np.asarray(v) for k, v in inputs.items()}
    f = np.float32

    def by_chunk(v):
        v = v.reshape(v.shape[:-1] + (-1, P))
        return np.ascontiguousarray(np.moveaxis(v, -1, 0))

    def columns(g):
        tag, w1, w2 = g["tag"], a["w_in"], a["w_in_2"][0]
        if tag in ("q", "k", "v", "g"):
            at = 4 * COLS * ("diff", "sb", "fox").index(g["kind"]) + COLS * "qkvg".index(tag)
            return w1[g["l"]][:, at:at + COLS]
        if tag == "o":
            r = COLS * ("diff", "sb", "fox").index(g["kind"])
            return a["w_out"][g["l"]][r:r + COLS, g["m"] * COLS:(g["m"] + 1) * COLS]
        if tag in ("q2", "k2", "v2"):
            at = 2 * D + G2 * COLS * ("q2", "k2", "v2").index(tag) + COLS * g["g"]
            return w2[:, at:at + COLS]
        if tag == "ffn":
            h = slice(g["m"] * COLS // 2, (g["m"] + 1) * COLS // 2)
            return np.concatenate([a["w_ffn_gate_2"][0][:, h], a["w_ffn_up_2"][0][:, h]], axis=1)
        c = slice(g["m"] * COLS, (g["m"] + 1) * COLS)
        if tag == "xr":
            return w2[:, c]
        if tag == "gr":
            return w2[:, D:2 * D][:, c]
        if tag == "gate":
            at = 2 * D + 3 * G2 * COLS + D * g["which"]
            return w2[:, at:at + D][:, c]
        if tag == "mix":
            return (a["w_attn_proj_2"] if g["which"] else a["w_lru_proj_2"])[0][:, c]
        if tag == "o2":
            return a["w_out_2"][0][:, c]
        return a["w_ffn_down_2"][0][:, c]

    stream = np.empty((NB, P, BC, COLS), f)
    for b, (gi, k) in enumerate(BLOCKS):
        w = columns(GROUPS[gi])[k * BC * P:(k + 1) * BC * P]
        stream[b] = w.reshape(BC, P, COLS).transpose(1, 0, 2)

    q, k = np.arange(P)[:, None], np.arange(P)[None, :]
    seen = {"causal": k <= q, "strict": k < q, "chunk": k // 64 <= q // 64, "prev": k >= q,
            "mod4d": (k <= q) & ((q - k) % 4 == 0), "mod4": (q - k) % 4 == 0,
            "mod16d": (k <= q) & ((q - k) % 16 == 0), "mod16": (q - k) % 16 == 0}
    masks = np.stack([np.where(seen[m], 0.0, NEG) for m in MASKS] + [np.eye(P)]).astype(ml_dtypes.bfloat16)
    sel = np.zeros((P, 8), f)
    sel[np.arange(8), np.arange(8)] = 1
    sel[32 + np.arange(8), np.arange(8)] = 1
    freq1 = f(500000.0) ** (-np.arange(0, ROT1, 2, dtype=f) / f(ROT1))
    freq2 = f(500000.0) ** (-np.arange(0, ROT2, 2, dtype=f) / f(ROT2))
    angle = np.arange(S, dtype=f)[:, None] * freq1[None]
    rope1 = np.stack([np.cos(angle), np.sin(angle)]).astype(f).reshape(2, TT, P, ROT1 // 2).transpose(2, 0, 1, 3)

    w_gates = np.zeros((P, 2, DC, P), f)
    for w, name in enumerate(("w_rg_2", "w_ig_2")):
        blocks = a[name][0].reshape(DC, 2, 64, 64)
        for h in range(2):
            w_gates[64 * h:64 * h + 64, w, :, 64 * h:64 * h + 64] = blocks[:, h].transpose(1, 0, 2)

    given = {
        "x": a["x"],
        "wstream": stream.reshape(NB, P, BC * COLS),
        "w_ff": a["w_in"][:, :, 12 * COLS:].reshape(DEPTH, DC, P, 8).transpose(2, 0, 1, 3),
        "f_bias": a["forget_bias"].T,
        "lam_vec": np.broadcast_to(a["diff_lambda"][None], (P, DEPTH, 4, HD)),
        "subln": a["diff_subln"].T,
        "gains": by_chunk(np.concatenate([a["pre_norm"], a["pre_mix_norm_2"], a["pre_ffn_norm_2"]])),
        "post_gains": np.concatenate([a["post_norm"], a["post_mix_norm_2"], a["post_ffn_norm_2"]]),
        "masks": masks.transpose(1, 0, 2),
        "ident_in": np.eye(P, dtype=f),
        "sel_in": sel,
        "rope1": rope1,
        "positions": a["positions_2"].reshape(TT, P).T,
        "inv_freq": np.broadcast_to(freq2[None], (P, ROT2 // 2)),
        "conv_w": by_chunk(a["conv_w_2"][0]).transpose(0, 2, 1),
        "conv_b": by_chunk(a["conv_b_2"][0]),
        "w_gates": w_gates.reshape(P, 2 * DC, P),
        "b_gates": by_chunk(np.concatenate([a["b_rg_2"], a["b_ig_2"]])),
        "lru_lambda": by_chunk(a["lru_lambda_2"][0]),
    }
    nc = bacc.Bacc("TRN2", target_bir_lowering=False, num_devices=1)
    args = {}
    for name, v in given.items():
        given[name] = v = np.ascontiguousarray(v)
        args[name] = nc.dram_tensor(name, v.shape, mybir.dt.from_np(v.dtype), kind="ExternalInput").ap()
    args["x_spill"] = nc.dram_tensor("x_spill", (P, TT, D), mybir.dt.float32, kind="Internal").ap()
    args["out"] = nc.dram_tensor("out", (1, S, D), mybir.dt.float32, kind="ExternalOutput").ap()
    build(nc, **args)
    return run_bass_kernel_spmd(nc, [given], core_ids=[0]).results[0]["out"]
```
